# Optimizing a Trainium2 kernel written in Bass

```python
import jax, jax.numpy as jnp
from jax import lax
import numpy as np

D_MODEL = 1024
BATCH = 1
SEQ = 512
DEPTH = 2

CHUNK = 64
N_EVEN = (DEPTH + 1) // 2
N_ODD = DEPTH // 2

LRU_WIDTH = 512
LRU_BLOCKS = 8
LRU_BLOCK = LRU_WIDTH // LRU_BLOCKS
LRU_CONV = 4
LRU_C = 8.0
SB_HEADS = 8
SB_HEAD_DIM = 64
SB_WIDTH = SB_HEADS * SB_HEAD_DIM
SB_QBLOCK = 128
EVEN_IN = 2 * LRU_WIDTH + 3 * SB_WIDTH
EVEN_MIX = LRU_WIDTH + SB_WIDTH
SW_HEADS = 16
SW_KV_HEADS = 4
SW_GROUPS = SW_HEADS // SW_KV_HEADS
SW_HEAD_DIM = 64
SW_WINDOW = 128
SW_WINDOW_CHUNKS = SW_WINDOW // CHUNK
ODD_IN = (SW_HEADS + 2 * SW_KV_HEADS) * SW_HEAD_DIM
ROPE_THETA = 10000.0
D_FF = 2816
FFN_CONV = 3
RMS_EPS = 1e-6

kernel_name = "hybrid_rglru_stickbreak_swa_convffn"

def rms_norm(x, g):
    xf = x.astype(jnp.float32)
    y = xf * lax.rsqrt(jnp.mean(xf * xf, axis=-1, keepdims=True) + RMS_EPS) * g.astype(jnp.float32)
    return y.astype(x.dtype)

def causal_dwconv(x, w, b):
    K = w.shape[0]
    S = x.shape[1]
    xp = jnp.pad(x, ((0, 0), (K - 1, 0), (0, 0)))
    y = xp[:, 0:S] * w[0]
    for k in range(1, K):
        y = y + xp[:, k:k + S] * w[k]
    return y + b

def rope(x, pos):
    half = x.shape[-1] // 2
    inv = ROPE_THETA ** (-jnp.arange(half, dtype=jnp.float32) / half)
    ang = pos.astype(jnp.float32)[..., None] * inv
    cos = jnp.cos(ang)[:, :, None, :]
    sin = jnp.sin(ang)[:, :, None, :]
    xf = x.astype(jnp.float32)
    x1, x2 = xf[..., :half], xf[..., half:]
    return jnp.concatenate([x1 * cos - x2 * sin, x2 * cos + x1 * sin], axis=-1).astype(x.dtype)

def rglru(x, w_a, b_a, w_x, b_x, lam):
    B, S, W = x.shape
    xf = x.astype(jnp.float32)
    xb = xf.reshape(B, S, LRU_BLOCKS, LRU_BLOCK)
    r = jax.nn.sigmoid(jnp.einsum('bsnc,ncd->bsnd', xb, w_a.astype(jnp.float32)) + b_a).reshape(B, S, W)
    i = jax.nn.sigmoid(jnp.einsum('bsnc,ncd->bsnd', xb, w_x.astype(jnp.float32)) + b_x).reshape(B, S, W)
    log_a = -LRU_C * r * jax.nn.softplus(-lam.astype(jnp.float32))
    a = jnp.exp(log_a)
    u = jnp.sqrt(-jnp.expm1(2.0 * log_a)) * (i * xf)

    def combine(left, right):
        a1, b1 = left
        a2, b2 = right
        return a1 * a2, a2 * b1 + b2

    _, h = lax.associative_scan(combine, (a, u), axis=1)
    return h.astype(x.dtype)

def stick_breaking(q, k, v):
    B, S, _ = q.shape
    q = q.reshape(B, S, SB_HEADS, SB_HEAD_DIM).transpose(0, 2, 1, 3)
    k = k.reshape(B, S, SB_HEADS, SB_HEAD_DIM).transpose(0, 2, 1, 3)
    v = v.reshape(B, S, SB_HEADS, SB_HEAD_DIM).transpose(0, 2, 1, 3)
    nqb = S // SB_QBLOCK
    qb = q.reshape(B, SB_HEADS, nqb, SB_QBLOCK, SB_HEAD_DIM).transpose(2, 0, 1, 3, 4)
    starts = jnp.arange(nqb, dtype=jnp.int32) * SB_QBLOCK
    key_pos = jnp.arange(S, dtype=jnp.int32)
    scale = SB_HEAD_DIM ** -0.5

    def one_block(args):
        q_blk, start = args
        z = jnp.einsum('bhqd,bhsd->bhqs', q_blk, k).astype(jnp.float32) * scale
        t = start + jnp.arange(SB_QBLOCK, dtype=jnp.int32)
        mask = key_pos[None, :] < t[:, None]
        sp = jnp.where(mask, jax.nn.softplus(z), 0.0)
        log_w = jax.nn.log_sigmoid(z) - (lax.cumsum(sp, axis=3, reverse=True) - sp)
        w = jnp.where(mask, jnp.exp(log_w), 0.0)
        return jnp.einsum('bhqs,bhsd->bhqd', w.astype(v.dtype), v)

    o = lax.map(one_block, (qb, starts))
    return o.transpose(1, 0, 3, 2, 4).reshape(B, S, SB_WIDTH)

def even_mixer(h, w_in, conv_w, conv_b, w_a, b_a, w_x, b_x, lam, w_out):
    u = h @ w_in
    o1 = LRU_WIDTH
    o2 = o1 + LRU_WIDTH
    o3 = o2 + SB_WIDTH
    o4 = o3 + SB_WIDTH
    xr, gr, q, k, v = u[..., :o1], u[..., o1:o2], u[..., o2:o3], u[..., o3:o4], u[..., o4:]
    xr = causal_dwconv(xr, conv_w, conv_b)
    y_a = rglru(xr, w_a, b_a, w_x, b_x, lam) * jax.nn.gelu(gr, approximate=True)
    y_b = stick_breaking(q, k, v)
    return jnp.concatenate([y_a, y_b], axis=-1) @ w_out

def odd_mixer(h, positions, w_qkv, sinks, w_o):
    B, S, _ = h.shape
    nc = S // CHUNK
    u = h @ w_qkv
    nq = SW_HEADS * SW_HEAD_DIM
    nk = SW_KV_HEADS * SW_HEAD_DIM
    q = rope(u[..., :nq].reshape(B, S, SW_HEADS, SW_HEAD_DIM), positions)
    k = rope(u[..., nq:nq + nk].reshape(B, S, SW_KV_HEADS, SW_HEAD_DIM), positions)
    v = u[..., nq + nk:].reshape(B, S, SW_KV_HEADS, SW_HEAD_DIM)
    q = q.reshape(B, nc, CHUNK, SW_KV_HEADS, SW_GROUPS, SW_HEAD_DIM)
    k = k.reshape(B, nc, CHUNK, SW_KV_HEADS, SW_HEAD_DIM)
    v = v.reshape(B, nc, CHUNK, SW_KV_HEADS, SW_HEAD_DIM)
    pad = SW_WINDOW_CHUNKS - 1
    kp = jnp.pad(k, ((0, 0), (pad, 0), (0, 0), (0, 0), (0, 0)))
    vp = jnp.pad(v, ((0, 0), (pad, 0), (0, 0), (0, 0), (0, 0)))
    k_band = jnp.concatenate([kp[:, i:i + nc] for i in range(SW_WINDOW_CHUNKS)], axis=2)
    v_band = jnp.concatenate([vp[:, i:i + nc] for i in range(SW_WINDOW_CHUNKS)], axis=2)
    scores = jnp.einsum('bcqkgd,bcskd->bckgqs', q, k_band).astype(jnp.float32) * (SW_HEAD_DIM ** -0.5)
    band_chunk = jnp.arange(nc)[:, None] - pad + jnp.arange(SW_WINDOW_CHUNKS)[None, :]
    valid = jnp.repeat(band_chunk >= 0, CHUNK, axis=1)
    scores = jnp.where(valid[None, :, None, None, None, :], scores, jnp.finfo(jnp.float32).min)
    sink = sinks.astype(jnp.float32).reshape(SW_KV_HEADS, SW_GROUPS)[None, None, :, :, None, None]
    sink = jnp.broadcast_to(sink, scores.shape[:-1] + (1,))
    p = jax.nn.softmax(jnp.concatenate([scores, sink], axis=-1), axis=-1)[..., :-1]
    o = jnp.einsum('bckgqs,bcskd->bcqkgd', p.astype(v.dtype), v_band)
    return o.reshape(B, S, nq) @ w_o

def conv_ffn(h, w_up, conv_w, conv_b, w_down):
    u = causal_dwconv(h @ w_up, conv_w, conv_b)
    g, val = u[..., :D_FF], u[..., D_FF:]
    return (jax.nn.gelu(g, approximate=True) * val) @ w_down

def setup_inputs(seed: int = 0) -> dict:
    key = jax.random.key(seed)
    ks = jax.random.split(key, 24)
    f32 = jnp.float32

    def nrm(k, shape, fan_in):
        return jax.random.normal(k, shape, f32) * (fan_in ** -0.5)

    def small(k, shape, s=0.01):
        return jax.random.normal(k, shape, f32) * s

    x = jax.random.normal(ks[0], (BATCH, SEQ, D_MODEL), f32)
    positions = jnp.broadcast_to(jnp.arange(SEQ, dtype=jnp.int32)[None, :], (BATCH, SEQ))
    even_w_in = nrm(ks[1], (N_EVEN, D_MODEL, EVEN_IN), D_MODEL)
    even_conv_w = nrm(ks[2], (N_EVEN, LRU_CONV, LRU_WIDTH), LRU_CONV)
    even_conv_b = small(ks[3], (N_EVEN, LRU_WIDTH))
    lru_w_a = nrm(ks[4], (N_EVEN, LRU_BLOCKS, LRU_BLOCK, LRU_BLOCK), LRU_BLOCK)
    lru_b_a = small(ks[5], (N_EVEN, LRU_BLOCKS, LRU_BLOCK))
    lru_w_x = nrm(ks[6], (N_EVEN, LRU_BLOCKS, LRU_BLOCK, LRU_BLOCK), LRU_BLOCK)
    lru_b_x = small(ks[7], (N_EVEN, LRU_BLOCKS, LRU_BLOCK))
    a_c = jax.random.uniform(ks[8], (N_EVEN, LRU_WIDTH), f32, minval=0.9, maxval=0.999)
    a0 = a_c ** (1.0 / LRU_C)
    lru_lambda = jnp.log(a0) - jnp.log1p(-a0)
    even_w_out = nrm(ks[9], (N_EVEN, EVEN_MIX, D_MODEL), EVEN_MIX)
    odd_w_qkv = nrm(ks[10], (N_ODD, D_MODEL, ODD_IN), D_MODEL)
    odd_sinks = small(ks[11], (N_ODD, SW_HEADS), 0.5)
    odd_w_o = nrm(ks[12], (N_ODD, SW_HEADS * SW_HEAD_DIM, D_MODEL), SW_HEADS * SW_HEAD_DIM)
    ffn_w_up = nrm(ks[13], (DEPTH, D_MODEL, 2 * D_FF), D_MODEL)
    ffn_conv_w = nrm(ks[14], (DEPTH, FFN_CONV, 2 * D_FF), FFN_CONV)
    ffn_conv_b = small(ks[15], (DEPTH, 2 * D_FF))
    ffn_w_down = nrm(ks[16], (DEPTH, D_FF, D_MODEL), D_FF)
    norm_mix_pre = 1.0 + small(ks[17], (DEPTH, D_MODEL), 0.05)
    norm_mix_post = 1.0 + small(ks[18], (DEPTH, D_MODEL), 0.05)
    norm_ffn_pre = 1.0 + small(ks[19], (DEPTH, D_MODEL), 0.05)
    norm_ffn_post = 1.0 + small(ks[20], (DEPTH, D_MODEL), 0.05)
    return {"x": x, "positions": positions,
            "even_w_in": even_w_in, "even_conv_w": even_conv_w, "even_conv_b": even_conv_b,
            "lru_w_a": lru_w_a, "lru_b_a": lru_b_a, "lru_w_x": lru_w_x, "lru_b_x": lru_b_x,
            "lru_lambda": lru_lambda, "even_w_out": even_w_out,
            "odd_w_qkv": odd_w_qkv, "odd_sinks": odd_sinks, "odd_w_o": odd_w_o,
            "ffn_w_up": ffn_w_up, "ffn_conv_w": ffn_conv_w, "ffn_conv_b": ffn_conv_b, "ffn_w_down": ffn_w_down,
            "norm_mix_pre": norm_mix_pre, "norm_mix_post": norm_mix_post,
            "norm_ffn_pre": norm_ffn_pre, "norm_ffn_post": norm_ffn_post}

def reference(x, positions, even_w_in, even_conv_w, even_conv_b, lru_w_a, lru_b_a, lru_w_x, lru_b_x,
              lru_lambda, even_w_out, odd_w_qkv, odd_sinks, odd_w_o, ffn_w_up, ffn_conv_w, ffn_conv_b,
              ffn_w_down, norm_mix_pre, norm_mix_post, norm_ffn_pre, norm_ffn_post):
    for layer in range(DEPTH):
        j = layer // 2
        h = rms_norm(x, norm_mix_pre[layer])
        if layer % 2 == 0:
            m = even_mixer(h, even_w_in[j], even_conv_w[j], even_conv_b[j], lru_w_a[j], lru_b_a[j],
                           lru_w_x[j], lru_b_x[j], lru_lambda[j], even_w_out[j])
        else:
            m = odd_mixer(h, positions, odd_w_qkv[j], odd_sinks[j], odd_w_o[j])
        x = x + rms_norm(m, norm_mix_post[layer])
        h = rms_norm(x, norm_ffn_pre[layer])
        f = conv_ffn(h, ffn_w_up[layer], ffn_conv_w[layer], ffn_conv_b[layer], ffn_w_down[layer])
        x = x + rms_norm(f, norm_ffn_post[layer])
    return x


_drawn_inputs = setup_inputs


def setup_inputs(seed=0):
    import zlib

    import numpy as np

    out = dict(_drawn_inputs(seed))
    spreads = {}
    factors = {'lru_b_a': 38.337, 'lru_b_x': 28.481, 'odd_sinks': 8.0, 'ffn_conv_b': 3.924}
    for name, (base, spread) in spreads.items():
        noise = np.random.default_rng([zlib.crc32(name.encode()), seed]).standard_normal(out[name].shape)
        drawn = base * np.exp(spread * noise) if base else spread * noise
        out[name] = __import__('jax').numpy.asarray(drawn.astype(out[name].dtype))
    for name, factor in factors.items():
        out[name] = (out[name] * factor).astype(out[name].dtype)
    return out
```

```python
from contextlib import ExitStack

import numpy as np
import concourse.bass as bass
from concourse import mybir

F32 = mybir.dt.float32
F32R = mybir.dt.float32r
BF16 = mybir.dt.bfloat16
I32 = mybir.dt.int32
ALU = mybir.AluOpType
ACT = mybir.ActivationFunctionType
AX = mybir.AxisListType

P = 128
T = 512
D = 1024
DT = D // P
TT = T // P
LRU = 512
LT = LRU // P
HD = 64
SB_HEADS = 8
F = 2816
FT = F // P
CHUNK = 64
NCH = T // CHUNK
KV = 4
EPS = 1e-6
SCALE = HD ** -0.5
MASKED = -1e30

RING = 3
UK = 8
DOWN_K = [(0, 8), (8, 16), (16, FT)]
N_IN, N_OUT, N_UP, N_DOWN, N_QKV = 10, 4, FT, 4 * len(DOWN_K), 6
U_IN = 0
U_OUT = [N_IN, 0]
U_UP = [U_OUT[0] + N_OUT, 0]
U_DOWN = [U_UP[0] + N_UP, 0]
U_QKV = U_DOWN[0] + N_DOWN
U_OUT[1] = U_QKV + N_QKV
U_UP[1] = U_OUT[1] + N_OUT
U_DOWN[1] = U_UP[1] + N_UP
N_UNITS = U_DOWN[1] + N_DOWN
G_SHIFT = N_DOWN - 4
N_SUMS = DT - 3

V_CONV = 64
V_CONVB, V_BA, V_BX, V_LAM = V_CONV + 16, V_CONV + 20, V_CONV + 24, V_CONV + 28
V_ROWS0 = V_LAM + 4
V_ROWSF = 4 * 2 * FT


def group_of(u):
    shift = 0
    for layer in range(2):
        if u >= U_DOWN[layer] + N_DOWN:
            shift += G_SHIFT
        elif u >= U_DOWN[layer]:
            return U_DOWN[layer] - shift + (u - U_DOWN[layer]) // len(DOWN_K)
    return u - shift


def dmas_of(u):
    for layer in range(2):
        if U_UP[layer] <= u < U_DOWN[layer]:
            return 2
    return 1


def loaded_at(u):
    return 16 * sum(dmas_of(v) for v in range(u % RING, u + 1, RING))


def build(nc, io, out):
    es = ExitStack()
    sem_names = {}

    def sem(name):
        sem_names[name] = es.enter_context(nc.semaphore(name))
        return sem_names[name]

    base = (nc.sbuf_base + 31) // 32 * 32
    where = [base]

    def at(name, shape, dt, offset):
        return nc.alloc_sbuf_tensor_at(name, shape, dt, offset=offset)

    def size(shape, dt):
        n = 2 if dt == BF16 else 4
        for s in shape[1:]:
            n *= s
        return (n + 31) // 32 * 32

    def place(name, shape, dt):
        t = at(name, shape, dt, where[0])
        where[0] += size(shape, dt)
        return t

    w_raw, w_lo, w_hi = [], [], []
    for s in range(RING):
        w_lo.append(at(f"w_lo{s}", [P, UK, 2, P], F32R, where[0]))
        w_raw.append(place(f"w_raw{s}", [P, UK, 2, P], F32))
        w_hi.append(place(f"w_hi{s}", [P, UK, 2, P], F32R))
    x = place("x", [P, DT, T], F32)
    m = at("m", [P, DT, T], F32, where[0])
    hx_hi = place("hx_hi", [P, DT, T], F32R)
    hx_lo = place("hx_lo", [P, DT, T], F32R)
    const = place("const", [P, 4 * P + 2], F32)
    ident, ones, tri, mask = (const[:, P * i:P * i + P] for i in range(4))
    inv_freq, rope_sign = const[:, 4 * P:4 * P + 1], const[:, 4 * P + 1:4 * P + 2]
    tri_r = place("tri_r", [P, P], F32R)
    ones_r = place("ones_r", [P, P], F32R)
    ident_b = place("ident_b", [P, P], BF16)
    mask_b = place("mask_b", [P, P], BF16)
    vec = place("vec", [P, V_ROWS0 + 2 * V_ROWSF], F32)
    nlam = place("nlam", [P, LT], F32)
    plam = place("plam", [P, LT], F32)
    narrow = place("narrow", [P, 10, 8], F32)
    std = place("std", [P, TT], F32)
    rcol = place("rcol", [P, TT], F32)
    sink = place("sink", [P, 8], F32)
    sink_row = place("sink_row", [P, 16], F32)
    rbc = place("rbc", [P, T], F32)
    cos_t = place("cos_t", [P, T], F32)
    sin_t = place("sin_t", [P, T], F32)
    sumsq = place("sumsq", [P, T], F32)
    tmp0 = where[0]
    ug = place("ug", [P, T], F32)
    uv = place("uv", [P, T], F32)
    cg = place("cg", [P, T], F32)
    cv = place("cv", [P, T], F32)
    big0 = where[0]
    g_hi = place("g_hi", [P, FT, T], F32R)
    g_lo = place("g_lo", [P, FT, T], F32R)
    assert where[0] <= nc.sbuf_usable_end, (where[0], nc.sbuf_usable_end)
    sq = [at(f"sq{b}", [P, T], F32, tmp0 + 2 * b * T * 4) for b in range(2)]
    diag = at("diag", [P, TT, P], F32, tmp0 + T * 4)

    class big:
        at_ = big0

    def inbig(name, shape, dt):
        t = at(name, shape, dt, big.at_)
        big.at_ += size(shape, dt)
        assert big.at_ <= where[0], name
        return t

    x_in = inbig("x_in", [P, TT, D], F32)
    vrow = inbig("vrow", [P, 5, P], F32)
    pos_i = inbig("pos_i", [P, T], I32)
    ang = inbig("ang", [P, T], F32)
    turns = inbig("turns", [P, T], F32)
    angc = inbig("angc", [P, T], F32)
    start_end = big.at_
    gate_w = at("gate_w", [P, 2, LT, P], F32, start_end)
    big.at_ = big0
    y_hi = inbig("y_hi", [P, DT, T], F32R)
    y_lo = inbig("y_lo", [P, DT, T], F32R)
    mix0 = big.at_
    assert start_end + 2 * LT * P * 4 <= mix0
    lru_a = at("lru_a", [P, LT, T], F32, big0 + LT * T * 4)
    lru_th = at("lru_th", [P, LT, T], F32, big0 + (DT + LT) * T * 4)
    qT = inbig("qT", [P, LT, T], F32)
    kT = inbig("kT", [P, LT, T], F32)
    v0 = inbig("v0", [P, TT, LRU], F32)
    att0 = big.at_
    xc = inbig("xc", [P, LT, T], F32)
    gr = inbig("gr", [P, LT, T], F32)
    lru_r = inbig("lru_r", [P, LT, T], F32)
    lru_i = inbig("lru_i", [P, LT, T], F32)
    big.at_ = att0
    SPAN = sum(T - P * j for j in range(TT))
    OFF = [0, T, 2 * T, T + (T - P)]
    z_s = [inbig(f"z_s{b}", [P, SPAN], F32) for b in range(3)]
    sp_lo = [at(f"sp_lo{b}", [P, SPAN], F32R, big.at_ + b * SPAN * 4) for b in range(2)]
    sp = [inbig(f"sp{b}", [P, SPAN], F32) for b in range(2)]
    sp_hi = [inbig("sp_hi0", [P, SPAN], F32R), at("sp_hi1", [P, SPAN], F32R, tmp0)]
    big.at_ = mix0
    qr = inbig("qr", [P, KV, NCH, 2, CHUNK], F32)
    kr = inbig("kr", [P, KV, T], F32)
    v1 = inbig("v1", [P, TT, KV * HD], F32)
    v1s = inbig("v1s", [P, TT, KV * HD], F32)
    rp = [inbig(f"rp{b}", [P, T], F32) for b in range(2)]
    rsw = [inbig(f"rsw{b}", [P, T], F32) for b in range(2)]
    prob = [inbig(f"prob{b}", [P, 8, P], F32) for b in range(2)]
    probT = [inbig(f"probT{b}", [P, 8, P], F32) for b in range(2)]
    out_s = at("out_s", [P, TT, D], F32, big0)

    ps = es.enter_context(nc.psum_tensor("ps", [P, 8 * T], F32))

    def bank(b, n=1):
        return ps[:, T * b:T * (b + n)]

    def group_banks(g):
        return 2 * (g % 3)

    const_in, vec_in, pos_in, gates_in, sink_in = (sem(n) for n in (
        "const_in", "vec_in", "pos_in", "gates_in", "sink_in"))
    x_loaded = [sem(f"x_loaded{q}") for q in range(4)]
    w_loaded = [sem(f"w_loaded{s}") for s in range(RING)]
    w_hi_done, w_lo_done, unit_done, group_evac = (sem(n) for n in (
        "w_hi_done", "w_lo_done", "unit_done", "group_evac"))
    zeroed, consts_cast, vec_mm, vec_done, xt_mm, xt_copied = (sem(n) for n in (
        "zeroed", "consts_cast", "vec_mm", "vec_done", "xt_mm", "xt_copied"))
    hx_hi_done, hx_ready, post_t, x_new, m_copied = (sem(n) for n in (
        "hx_hi_done", "hx_ready", "post_t", "x_new", "m_copied"))
    sq_done, sum_done, ms_mm, std_done, rcol_done, diag_done, bc_mm, rbc_done = (sem(n) for n in (
        "sq_done", "sum_done", "ms_mm", "std_done", "rcol_done", "diag_done", "bc_mm", "rbc_done"))
    setup_v, setup_a = sem("setup_v"), sem("setup_a")
    xc_center, xc_tap, gate_mm, gate_act, lru_act, lru_dve = (sem(n) for n in (
        "xc_center", "xc_tap", "gate_mm", "gate_act", "lru_act", "lru_dve"))
    y_hi_done, y_ready = sem("y_hi_done"), sem("y_ready")
    z_mm, z_copied, abs_done, exp_done, ln_done, sp_done, sp_hi_done, sp_lo_done = (sem(n) for n in (
        "z_mm", "z_copied", "abs_done", "exp_done", "ln_done", "sp_done", "sp_hi_done", "sp_lo_done"))
    cum_mm, t_done, w_done, av_mm = (sem(n) for n in ("cum_mm", "t_done", "w_done", "av_mm"))
    scaled, center, tapped, gelu_done, prod_done, g_hi_done, g_ready = (sem(n) for n in (
        "scaled", "center", "tapped", "gelu_done", "prod_done", "g_hi_done", "g_ready"))
    rope_sw = [sem(f"rope_swapped{b}") for b in range(2)]
    rope_raw, rope_mul, rope_done, v_shift, v_raw = (sem(n) for n in (
        "rope_raw", "rope_mul", "rope_done", "v_shift", "v_raw"))
    k_copied = sem("k_copied")
    s_mm, smax_done, negm_done, p_done, ex_done, sw_step, pn_done, pt_mm, pt_copied, o_mm = (sem(n) for n in (
        "s_mm", "smax_done", "negm_done", "p_done", "ex_done", "sw_step", "pn_done", "pt_mm", "pt_copied", "o_mm"))
    out_mm, out_copied, stored = sem("out_mm"), sem("out_copied"), sem("stored")

    PHASES = [U_IN, U_OUT[0], U_UP[0], U_DOWN[0], U_QKV, U_OUT[1], U_UP[1], U_DOWN[1]]
    FFN_TAPS = V_ROWS0

    def ffn_vec(layer, what, j):
        return FFN_TAPS + V_ROWSF * layer + 2 * FT * what + j

    def gain(which, layer, i):
        c = 16 * which + 8 * layer + i
        return vec[:, c:c + 1]

    def col(c):
        return vec[:, bass.ds(c, 1)] if not isinstance(c, int) else vec[:, c:c + 1]

    def tile_(t, i):
        return t[:, bass.ds(i, 1), :].rearrange("p a t -> p (a t)") if not isinstance(i, int) else t[:, i, :]

    def split_at(layer, u):
        return {0: u + 3, 1: u + 3, 2: None}.get(u - U_UP[layer], u + 2)

    block = es.enter_context(nc.Block())

    @block.sync
    def _(sp_):
        def slot_free(u, i=None, per=0):
            if i is not None:
                sp_.wait_ge(unit_done, i * per + (u - RING + 1))
            elif u >= RING:
                sp_.wait_ge(unit_done, u - RING + 1)

        def load(u, src, dst=None):
            s = u % RING
            sp_.dma_start(w_raw[s][:] if dst is None else dst, src).then_inc(w_loaded[s], 16)

        def cols(w, c0, n=2 * P):
            c = slice(c0, c0 + n) if isinstance(c0, int) else bass.ds(c0, n)
            return w[:, c].rearrange("(k p) n -> p k n", p=P)

        def whole(s, k=UK):
            return w_raw[s][:, 0:k].rearrange("p k b n -> p k (b n)")

        def load_cols(u, w, c0):
            slot_free(u)
            load(u, cols(w, c0), whole(u % RING))

        w_in, w_qkv = io["even_w_in"][0], io["odd_w_qkv"][0]
        order = [0, 256, 512, 768, 1024, 1280, 1536, 1792, 2048, 2304]
        sp_.dma_start(const[:], io["consts"]).then_inc(const_in, 16)
        xv = io["x"][0].rearrange("(t p) d -> p t d", p=P)
        for q in range(4):
            sp_.dma_start(x_in[:, :, 256 * q:256 * q + 256], xv[:, :, 256 * q:256 * q + 256]).then_inc(x_loaded[q], 16)
            if q == 0:
                sp_.wait_ge(zeroed, 1)
                row = 0
                rows = [(io[n].rearrange("l (i c) -> (l i) c", c=P), 16) for n in (
                    "norm_mix_pre", "norm_mix_post", "norm_ffn_pre", "norm_ffn_post")]
                rows.append((io["even_conv_w"][0].rearrange("k (i c) -> (k i) c", c=P), 16))
                rows.append((io["even_conv_b"][0].rearrange("(i c) -> i c", c=P), 4))
                rows.append((io["lru_b_a"][0].rearrange("(i a) c -> i (a c)", a=2), 4))
                rows.append((io["lru_b_x"][0].rearrange("(i a) c -> i (a c)", a=2), 4))
                rows.append((io["lru_lambda"][0].rearrange("(i c) -> i c", c=P), 4))
                for src, n in rows:
                    sp_.dma_start(vrow[row:row + n, 0, :], src).then_inc(vec_in, 16)
                    row += n
                for layer in range(2):
                    wv = io["ffn_conv_w"][layer].rearrange("k (i c) -> (k i) c", c=P)
                    bv = io["ffn_conv_b"][layer].rearrange("(i c) -> i c", c=P)
                    n = 2 * FT
                    sp_.dma_start(vrow[0:2 * n, 1 + 2 * layer, :], wv[0:2 * n]).then_inc(vec_in, 16)
                    sp_.dma_start(vrow[0:n, 2 + 2 * layer, :], wv[2 * n:3 * n]).then_inc(vec_in, 16)
                    sp_.dma_start(vrow[n:2 * n, 2 + 2 * layer, :], bv).then_inc(vec_in, 16)
            if q < 2:
                load_cols(q, w_in, order[q])
        load_cols(2, w_in, order[2])
        sp_.dma_start(pos_i[:], io["positions"][0:1, :].broadcast_to([P, T])).then_inc(pos_in, 16)
        sp_.dma_start(sink_row[:], io["odd_sinks"][0:1, :].broadcast_to([P, 16])).then_inc(sink_in, 16)
        sp_.wait_ge(zeroed, 2)
        for g, name in enumerate(("lru_w_a", "lru_w_x")):
            wv = io[name][0].rearrange("(i a) c d -> a c i d", a=2)
            for a in range(2):
                sp_.dma_start(gate_w[64 * a:64 * a + 64, g, :, 64 * a:64 * a + 64], wv[a]).then_inc(gates_in, 16)
        for u in range(3, N_IN):
            load_cols(u, w_in, order[u])

        for layer in range(2):
            if layer == 1:
                for j, c0 in enumerate((D, 0, 256)):
                    load_cols(U_QKV + j, w_qkv, c0)

                def swap(i):
                    for b in range(2):
                        sp_.wait_ge(rope_raw, 2 * i + b + 1)
                        for a in range(4):
                            c = a ^ 1
                            sp_.dma_start(rsw[b][32 * a:32 * a + 32, :], rp[b][32 * c:32 * c + 32, :]).then_inc(rope_sw[b], 16)

                load_cols(U_QKV + 3, w_qkv, 512)
                swap(0)
                load_cols(U_QKV + 4, w_qkv, 768)
                swap(1)
                load_cols(U_QKV + 5, w_qkv, D + KV * HD)
                swap(2)
                sp_.wait_ge(rope_done, 4)
                for kv in range(KV):
                    a, b = 64 * (kv % 2), 64 * (1 - kv % 2)
                    sp_.dma_start(kr[b:b + 64, kv, :], kr[a:a + 64, kv, :]).then_inc(k_copied, 16)
                for i in range(3, 5):
                    load_cols(U_OUT[layer] + i - 3, io["odd_w_o"][0], 256 * (i - 3))
                    swap(i)
                sp_.wait_ge(v_raw, 4)
                sp_.dma_start(v1s[0:64, 1:TT, :], v1[64:128, 0:TT - 1, :]).then_inc(v_shift, 16)
                sp_.dma_start(v1s[64:128, 1:TT, :], v1[0:64, 1:TT, :]).then_inc(v_shift, 16)
            w_o = (io["even_w_out"], io["odd_w_o"])[layer][0]
            for j in range(2 * layer, N_OUT):
                load_cols(U_OUT[layer] + j, w_o, 256 * j)
            w_up = io["ffn_w_up"][layer]

            def load_up(u, j, i=None):
                slot_free(u, i, RING)
                for b in range(2):
                    load(u, cols(w_up, j * P + F * b, P), w_raw[u % RING][:, :, b, :])

            for j in range(2):
                load_up(U_UP[layer] + j, j)
            with sp_.Fori(0, 6) as i:
                for j in range(RING):
                    load_up(U_UP[layer] + 2 + j, i * RING + (2 + j), i)
            for j in range(20, FT):
                load_up(U_UP[layer] + j, j)
            w_down = io["ffn_w_down"][layer]
            with sp_.Fori(0, 4) as i:
                for c, (k0, k1) in enumerate(DOWN_K):
                    u = U_DOWN[layer] + c
                    slot_free(u, i, RING)
                    src = w_down[k0 * P:k1 * P, bass.ds(i * 256, 256)].rearrange("(k p) n -> p k n", p=P)
                    load(u, src, whole(u % RING, k1 - k0))
        ov = out[0].rearrange("(t p) d -> p t d", p=P)
        for i in range(DT):
            sp_.wait_ge(out_copied, i + 1)
            sp_.dma_start(ov[:, :, P * i:P * i + P], out_s[:, :, P * i:P * i + P]).then_inc(stored, 16)
        sp_.wait_ge(stored, 16 * DT)

    @block.gpsimd
    def _(pool):
        pool.memset(vrow[:], 0.0).then_inc(zeroed, 1)
        pool.memset(gate_w[:], 0.0).then_inc(zeroed, 1)
        for n in range(8):
            for i in range(1, N_SUMS + 1):
                pool.wait_ge(sq_done, DT * n + i + 1)
                if i == 1:
                    if n:
                        pool.wait_ge(ms_mm, n)
                    ins = pool.tensor_tensor(sumsq[:], sq[0][:], sq[1][:], ALU.add)
                else:
                    pool.wait_ge(sum_done, N_SUMS * n + i - 1)
                    ins = pool.tensor_tensor(sumsq[:], sumsq[:], sq[i % 2][:], ALU.add)
                ins.then_inc(sum_done, 1)

    @block.scalar
    def _(act):
        def split_hi(u, k=UK, i=None, per=RING, cnt=0):
            s = u % RING
            at_ = loaded_at(u)
            act.wait_ge(w_loaded[s], at_ if i is None else i * cnt + at_)
            act.activation(w_hi[s][:, 0:k], w_raw[s][:, 0:k], ACT.Copy).then_inc(w_hi_done, 1)

        def square(n, i, src):
            if i >= 2:
                act.wait_ge(sum_done, N_SUMS * n + max(1, i - 2))
            elif n:
                act.wait_ge(ms_mm, n)
            act.activation(sq[i % 2][:], src, ACT.Square).then_inc(sq_done, 1)

        def root(n):
            act.wait_ge(ms_mm, n + 1)
            act.activation(std[:], bank(7)[:, 0:TT], ACT.Sqrt, scale=1.0 / D, bias=eps).then_inc(std_done, 1)

        eps = narrow[:, 9, 0:1]

        split_hi(0)
        act.wait_ge(vec_done, 1)
        for i in range(DT):
            act.wait_ge(xt_copied, i + 1)
            act.activation(hx_hi[:, i, :], x[:, i, :], ACT.Identity, scale=gain(0, 0, i)).then_inc(hx_hi_done, 1)
            square(0, i, x[:, i, :])
            if i == 1:
                split_hi(1)
        split_hi(2)
        root(0)
        act.wait_ge(setup_v, 1)
        act.activation(narrow[:, 1, 0:LT], narrow[:, 0, 0:LT], ACT.Exp, scale=-1.0).then_inc(setup_a, 1)

        def sines():
            act.wait_ge(setup_v, 2)
            act.activation(sin_t[:], ang[:], ACT.Sin).then_inc(setup_a, 1)
            act.activation(cos_t[:], angc[:], ACT.Sin).then_inc(setup_a, 1)

        for u in range(N_IN):
            g = group_of(u)
            if u < 2:
                act.wait_ge(group_evac, g + 1)
                for b in range(2):
                    t = 2 * u + b
                    act.activation(xc[:, t, :], (ug, uv)[b][:], ACT.Identity, scale=col(V_CONV + 12 + t),
                                   bias=col(V_CONVB + t)).then_inc(xc_center, 1)
            if u + 2 >= 3:
                split_hi(u + 2)
            if u == 2:
                sines()
            if 2 <= u < 6:
                t = u - 2
                for b, (dst, bias) in enumerate(((lru_r, V_BA), (lru_i, V_BX))):
                    act.wait_ge(gate_mm, 2 * t + b + 1)
                    act.activation(dst[:, t, :], bank(6 + b), ACT.Sigmoid, bias=col(bias + t)).then_inc(gate_act, 1)
            if u == 5:
                act.wait_ge(setup_v, 3)
                act.wait_ge(gate_act, 2 * LT)
                for t in range(LT):
                    act.activation(lru_a[:, t, :], lru_r[:, t, :], ACT.Exp, scale=nlam[:, t:t + 1]).then_inc(lru_act, 1)
                for t in range(LT):
                    act.activation(lru_th[:, t, :], lru_r[:, t, :], ACT.Tanh, scale=plam[:, t:t + 1]).then_inc(lru_act, 1)
            if u == 6:
                act.wait_ge(lru_dve, 3)
                act.activation(lru_r[:], lru_r[:], ACT.Sqrt).then_inc(lru_act, 1)
                act.activation(gr[:], gr[:], ACT.Gelu_apprx_tanh).then_inc(lru_act, 1)
                act.preload_act_table_set("natural_log_exp_and_others")
            if u == 7:
                act.wait_ge(lru_dve, 4 + LT + 1)
                act.activation(y_hi[:, 0:LT, :], lru_r[:], ACT.Copy).then_inc(y_hi_done, 1)


        def sb_softplus(h):
            b = h % 2
            act.wait_ge(z_copied, h + 1)
            if h >= 2:
                act.wait_ge(cum_mm, h - 1)
            act.activation(sp[b][:], z_s[h % 3][:], ACT.Abs).then_inc(abs_done, 1)
            act.wait_ge(abs_done, h + 1)
            act.activation(sp[b][:], sp[b][:], ACT.Exp, scale=-1.0).then_inc(exp_done, 1)
            act.wait_ge(exp_done, h + 1)
            act.activation(sp[b][:], sp[b][:], ACT.Ln, bias=1.0).then_inc(ln_done, 1)

        def sb_weights(h):
            act.wait_ge(t_done, h + 1)
            act.activation(z_s[h % 3][:], z_s[h % 3][:], ACT.Exp).then_inc(w_done, 1)

        def sb_out(ti):
            act.wait_ge(av_mm, 2 * ti + 2)
            act.activation(y_hi[:, LT + ti, :], bank(6 + ti % 2), ACT.Copy).then_inc(y_hi_done, 1)

        def sb_hi(h):
            act.wait_ge(sp_done, h + 1)
            act.activation(sp_hi[h % 2][:], sp[h % 2][:], ACT.Copy).then_inc(sp_hi_done, 1)

        sb_softplus(0)
        sb_hi(0)
        sb_softplus(1)
        for h in range(SB_HEADS):
            if h + 1 < SB_HEADS:
                sb_hi(h + 1)
            sb_weights(h)
            if h >= 2 and h % 2 == 0:
                sb_out(h // 2 - 1)
            if h == 1:
                split_hi(U_OUT[0] + 2)
            if h + 2 < SB_HEADS:
                sb_softplus(h + 2)
        sb_out(SB_HEADS // 2 - 1)

        def boundary(bi, n, which, layer, u):
            root(n)
            for i in range(DT):
                act.wait_ge(x_new, DT * bi + i + 1)
                act.activation(hx_hi[:, i, :], x[:, i, :], ACT.Identity, scale=gain(which, layer, i)).then_inc(hx_hi_done, 1)
                square(n + 1, i, x[:, i, :])
            split_hi(u + 2)
            root(n + 1)

        def out_projection(layer, n):
            for j in range(N_OUT):
                u = U_OUT[layer] + j
                split = j > 0
                for b in range(2):
                    m_squares(n, u, j, b)
                if split:
                    split_hi(u + 2)

        def m_squares(n, u, mp, b):
            if b == 0:
                act.wait_ge(m_copied, 4 * (n // 2) + mp + 1)
            else:
                act.wait_ge(group_evac, group_of(u) + 1)
            square(n, 2 * mp + b, m[:, 2 * mp + b, :])

        def ffn_up(layer, j, u, i=None):
            f = FT * layer + j
            g = group_of(u)
            act.wait_ge(scaled, f + 1)
            if i is not None or j or layer:
                act.wait_ge(prod_done, f)
            act.activation(cg[:], ug[:], ACT.Identity, scale=col(ffn_vec(layer, 2, j)), bias=col(ffn_vec(layer, 3, j))).then_inc(center, 1)
            act.wait_ge(group_evac, g + 1 if i is None else i * RING + (g + 1))
            if i is not None or j or layer:
                act.wait_ge(g_ready, f)
            act.activation(cv[:], uv[:], ACT.Identity, scale=col(ffn_vec(layer, 2, j + FT)), bias=col(ffn_vec(layer, 3, j + FT))).then_inc(center, 1)
            v = split_at(layer, u)
            if v is not None:
                split_hi(v, i=i, cnt=32)
            act.wait_ge(tapped, 4 * f + 3)
            act.activation(cg[:], cg[:], ACT.Gelu_apprx_tanh).then_inc(gelu_done, 1)
            act.wait_ge(prod_done, f + 1)
            act.activation(tile_(g_hi, j), cv[:], ACT.Copy).then_inc(g_hi_done, 1)

        def ffn(layer):
            for j in range(3):
                ffn_up(layer, j, U_UP[layer] + j)
            with act.Fori(0, 5) as i:
                for j in range(RING):
                    ffn_up(layer, i * RING + (3 + j), U_UP[layer] + 3 + j, i)
            for j in range(18, FT):
                ffn_up(layer, j, U_UP[layer] + j)
            for mp in range(4):
                for c in range(3):
                    u = U_DOWN[layer] + 3 * mp + c
                    if c == 2:
                        for b in range(2):
                            m_squares(4 * layer + 3, u, mp, b)
                    v = u + 2
                    if v < U_DOWN[layer] + N_DOWN:
                        k0, k1 = DOWN_K[(3 * mp + c + 2) % 3]
                        split_hi(v, k1 - k0)
                    elif v < N_UNITS:
                        split_hi(v)

        out_projection(0, 1)
        boundary(0, 1, 2, 0, U_UP[0])
        ffn(0)
        boundary(1, 3, 0, 1, U_QKV)
        for k in range(N_QKV):
            if k != 2:
                split_hi(U_QKV + k + (3 if k < 2 else 2))

        for c in range(NCH + 1):
            if c < NCH:
                kw = HD if c == 0 else P
                for e in range(8):
                    if e == 0:
                        act.wait_ge(negm_done, c + 1)
                        if c >= 2:
                            act.wait_ge(pt_mm, 2 * (c - 1))
                    bk = bank(2 * (c % 2), 2).rearrange("p (e k) -> p e k", k=P)
                    act.activation(prob[c % 2][:, e, 0:kw], bk[:, e, 0:kw], ACT.Exp, bias=narrow[:, 4 * (c % 2), e:e + 1],
                                   accum_out=narrow[:, 4 * (c % 2) + 1, e:e + 1]).then_inc(p_done, 1)
                act.activation(narrow[:, 4 * (c % 2) + 2, 0:8], narrow[:, 4 * (c % 2) + 3, 0:8], ACT.Exp).then_inc(ex_done, 1)
            if c == 1:
                split_hi(U_OUT[1] + 2)
            if c >= 1:
                d = c - 1
                kw = HD if d == 0 else P
                for q in range(2):
                    act.wait_ge(pt_mm, 2 * d + q + 1)
                    if d >= 2:
                        act.wait_ge(o_mm, d - 1)
                    act.activation(probT[d % 2][0:kw, 4 * q:4 * q + 4, :], bank(4 + q).rearrange("p (e k) -> p e k", k=P)[0:kw],
                                   ACT.Copy).then_inc(pt_copied, 1)
                act.wait_ge(o_mm, d + 1)
                act.activation(y_hi[:, :, CHUNK * d:CHUNK * d + CHUNK],
                               bank(6).rearrange("p (k t) -> p k t", t=CHUNK), ACT.Copy).then_inc(y_hi_done, 1)
        out_projection(1, 5)
        boundary(2, 5, 2, 1, U_UP[1])
        ffn(1)
        root(7)

    @block.vector
    def _(dve):
        def split_lo(u, k=UK, i=None):
            s = u % RING
            dve.wait_ge(w_hi_done, u + 1 if i is None else i * RING + (u + 1))
            dve.tensor_tensor(w_lo[s][:, 0:k], w_raw[s][:, 0:k], w_hi[s][:, 0:k], ALU.subtract).then_inc(w_lo_done, 1)

        def inverse_rms(n):
            dve.wait_ge(std_done, n + 1)
            if n:
                dve.wait_ge(diag_done, n)
            dve.reciprocal(rcol[:], std[:]).then_inc(rcol_done, 1)
            dve.wait_ge(rcol_done, n + 1)
            for t in range(TT):
                ins = dve.tensor_scalar(diag[:, t, :], ident, rcol[:, t:t + 1], None, ALU.mult)
            ins.then_inc(diag_done, 1)

        def spread(n):
            dve.wait_ge(bc_mm, n + 1)
            dve.tensor_copy(rbc[:], bank(6)).then_inc(rbc_done, 1)

        dve.memset(narrow[:, 9, 0:1], EPS)
        dve.wait_ge(const_in, 16)
        dve.tensor_copy(tri_r[:], tri)
        dve.tensor_copy(ones_r[:], ones)
        dve.tensor_copy(ident_b[:], ident)
        dve.tensor_copy(mask_b[:], mask).then_inc(consts_cast, 1)
        split_lo(0)
        dve.wait_ge(vec_mm, 1)
        dve.tensor_copy(vec[:], bank(5)[:, 0:V_ROWS0 + 2 * V_ROWSF]).then_inc(vec_done, 1)
        dve.wait_ge(vec_done, 1)
        for i in range(DT):
            dve.wait_ge(xt_mm, i + 1)
            dve.tensor_copy(x[:, i, :], bank(6 + i % 2)).then_inc(xt_copied, 1)
            dve.wait_ge(hx_hi_done, i + 1)
            dve.scalar_tensor_tensor(out=hx_lo[:, i, :], in0=x[:, i, :], scalar=gain(0, 0, i), in1=hx_hi[:, i, :],
                                     op0=ALU.mult, op1=ALU.subtract).then_inc(hx_ready, 1)
            if i == 1:
                split_lo(1)
        lam = vec[:, V_LAM:V_LAM + LT]
        dve.scalar_tensor_tensor(out=narrow[:, 0, 0:LT], in0=lam, scalar=-1.0, in1=lam, op0=ALU.mult, op1=ALU.max).then_inc(setup_v, 1)
        split_lo(2)
        inverse_rms(0)
        spread(0)

        chain = sem("setup_chain")
        made = [0]

        def step(ins):
            made[0] += 1
            ins.then_inc(chain, 1)
            dve.wait_ge(chain, made[0])

        def rotary_angles():
            c1 = 6.28125
            c2 = float(np.float32(np.int64((2 * np.pi - c1) * 2 ** 20) / 2.0 ** 20))
            c3 = float(2 * np.pi - c1 - c2)
            magic = 12582912.0
            pi = float(np.nextafter(np.float32(np.pi), np.float32(0)))
            dve.wait_ge(pos_in, 16)
            step(dve.tensor_copy(ang[:], pos_i[:]))
            step(dve.tensor_scalar(ang[:], ang[:], inv_freq, None, ALU.mult))
            step(dve.tensor_scalar(turns[:], ang[:], float(1 / (2 * np.pi)), magic, ALU.mult, ALU.add))
            step(dve.tensor_scalar(turns[:], turns[:], -magic, None, ALU.add))
            for c in (c1, c2, c3):
                step(dve.scalar_tensor_tensor(out=ang[:], in0=turns[:], scalar=-c, in1=ang[:], op0=ALU.mult, op1=ALU.add))
            step(dve.tensor_scalar(turns[:], ang[:], float(np.pi / 2), -2 * float(np.pi), ALU.is_gt, ALU.mult))
            step(dve.scalar_tensor_tensor(out=angc[:], in0=ang[:], scalar=float(np.pi / 2), in1=turns[:], op0=ALU.add, op1=ALU.add))
            step(dve.tensor_scalar(ang[:], ang[:], pi, -pi, ALU.min, ALU.max))
            dve.tensor_scalar(angc[:], angc[:], pi, -pi, ALU.min, ALU.max).then_inc(setup_v, 1)

        def softplus_lambda():
            e, s, s2, q = (narrow[:, r, 0:LT] for r in (1, 2, 3, 4))
            dve.wait_ge(setup_a, 1)
            step(dve.tensor_scalar(s, e, 2.0, None, ALU.add))
            step(dve.reciprocal(s, s))
            step(dve.tensor_tensor(s, s, e, ALU.mult))
            step(dve.tensor_tensor(s2, s, s, ALU.mult))
            step(dve.tensor_scalar(q, s2, 1.0 / 17, None, ALU.mult))
            for k in (15, 13, 11, 9, 7, 5, 3):
                step(dve.scalar_tensor_tensor(out=q, in0=q, scalar=1.0 / k, in1=s2, op0=ALU.add, op1=ALU.mult))
            step(dve.scalar_tensor_tensor(out=q, in0=q, scalar=1.0, in1=s, op0=ALU.add, op1=ALU.mult))
            step(dve.tensor_scalar(s, vec[:, V_LAM:V_LAM + LT], -1.0, 0.0, ALU.mult, ALU.max))
            step(dve.scalar_tensor_tensor(out=q, in0=q, scalar=2.0, in1=s, op0=ALU.mult, op1=ALU.add))
            step(dve.tensor_scalar(plam[:], q, 8.0, None, ALU.mult))
            dve.tensor_scalar(nlam[:], q, -8.0, None, ALU.mult).then_inc(setup_v, 1)

        def rotary_signs():
            dve.wait_ge(setup_a, 3)
            step(dve.tensor_scalar(sin_t[:], sin_t[:], rope_sign, None, ALU.mult))
            dve.wait_ge(sink_in, 16)
            v = sink_row[:].rearrange("p (k g h) -> p g k h", g=2, h=2)
            for g in range(2):
                step(dve.tensor_copy(sink[64 * g:64 * g + 64, :].rearrange("p (h k) -> p k h", h=2), v[64 * g:64 * g + 64, g]))

        def lru_inputs():
            dve.wait_ge(gate_act, 2 * LT)
            dve.tensor_tensor(lru_i[:], lru_i[:], xc[:], ALU.mult).then_inc(lru_dve, 1)
            dve.wait_ge(lru_act, 2 * LT)
            dve.tensor_tensor(lru_r[:], lru_a[:], lru_a[:], ALU.mult).then_inc(lru_dve, 1)
            dve.wait_ge(lru_dve, 2)
            dve.scalar_tensor_tensor(out=lru_r[:], in0=lru_r[:], scalar=1.0, in1=lru_th[:], op0=ALU.add, op1=ALU.mult).then_inc(lru_dve, 1)

        def lru_scan():
            dve.wait_ge(lru_act, 2 * LT + 1)
            dve.tensor_tensor(lru_i[:], lru_i[:], lru_r[:], ALU.mult).then_inc(lru_dve, 1)
            dve.wait_ge(lru_dve, 4)
            for t in range(LT):
                dve.tensor_tensor_scan(out=xc[:, t, :], data0=lru_a[:, t, :], data1=lru_i[:, t, :], initial=0.0,
                                       op0=ALU.mult, op1=ALU.add).then_inc(lru_dve, 1)
            dve.wait_ge(lru_act, 2 * LT + 2)
            dve.wait_ge(lru_dve, 4 + LT)
            dve.tensor_tensor(lru_r[:], xc[:], gr[:], ALU.mult).then_inc(lru_dve, 1)

        for u in range(N_IN):
            g = group_of(u)
            dve.wait_ge(unit_done, u + 1)
            if u == 0:
                dve.wait_ge(rbc_done, 1)
            b0 = group_banks(g)
            if u < 2:
                if u:
                    dve.wait_ge(xc_tap, 6 * u)
                for b in range(2):
                    ins = dve.tensor_tensor((ug, uv)[b][:], bank(b0 + b), rbc[:], ALU.mult)
                ins.then_inc(group_evac, 1)
                for s in range(1, 4):
                    for b in range(2):
                        t = 2 * u + b
                        if s == 1:
                            dve.wait_ge(xc_center, 2 * u + b + 1)
                        else:
                            dve.wait_ge(xc_tap, 6 * u + 2 * (s - 2) + b + 1)
                        dve.scalar_tensor_tensor(out=xc[:, t, s:], in0=(ug, uv)[b][:, 0:T - s], scalar=col(V_CONV + 4 * (3 - s) + t),
                                                 in1=xc[:, t, s:], op0=ALU.mult, op1=ALU.add).then_inc(xc_tap, 1)
            elif u < 8:
                dst = {1: gr, 2: qT, 3: kT}[u // 2]
                for b in range(2):
                    t = 2 * (u % 2) + b
                    if u // 2 == 2:
                        ins = dve.scalar_tensor_tensor(out=dst[:, t, :], in0=bank(b0 + b), scalar=SCALE, in1=rbc[:], op0=ALU.mult, op1=ALU.mult)
                    else:
                        ins = dve.tensor_tensor(dst[:, t, :], bank(b0 + b), rbc[:], ALU.mult)
                ins.then_inc(group_evac, 1)
            else:
                for t in range(TT):
                    c = T * b0 + 256 * t
                    ins = dve.tensor_scalar(v0[:, t, 256 * (u - 8):256 * (u - 8) + 256], ps[:, c:c + 256], rcol[:, t:t + 1], None, ALU.mult)
                ins.then_inc(group_evac, 1)
            if u + 2 >= 3:
                split_lo(u + 2)
            if u == 2:
                rotary_angles()
                softplus_lambda()
            if u == 3:
                rotary_signs()
            if u == 5:
                lru_inputs()
            if u == 6:
                lru_scan()
            if u == 7:
                dve.wait_ge(y_hi_done, 1)
                dve.tensor_tensor(y_lo[:, 0:LT, :], lru_r[:], y_hi[:, 0:LT, :], ALU.subtract).then_inc(y_ready, 1)
        def sb_z(h):
            dve.wait_ge(z_mm, h + 1)
            if h >= 3:
                dve.wait_ge(av_mm, h - 2)
            dve.tensor_copy(z_s[h % 3][:], bank(0, 3)[:, 0:SPAN]).then_inc(z_copied, 1)

        def sb_t(h):
            dve.wait_ge(cum_mm, h + 1)
            dve.tensor_tensor(z_s[h % 3][:], z_s[h % 3][:], bank(3, 3)[:, 0:SPAN], ALU.subtract).then_inc(t_done, 1)

        def sb_out(ti):
            dve.wait_ge(y_hi_done, 1 + ti + 1)
            dve.tensor_tensor(y_lo[:, LT + ti, :], bank(6 + ti % 2), y_hi[:, LT + ti, :], ALU.subtract).then_inc(y_ready, 1)

        dve.wait_ge(y_ready, 1)
        def sb_softplus(h):
            dve.wait_ge(ln_done, h + 1)
            dve.scalar_tensor_tensor(out=sp[h % 2][:], in0=z_s[h % 3][:], scalar=0.0, in1=sp[h % 2][:], op0=ALU.max, op1=ALU.add).then_inc(sp_done, 1)

        def sb_lo(h):
            dve.wait_ge(sp_hi_done, h + 1)
            dve.tensor_tensor(sp_lo[h % 2][:], sp[h % 2][:], sp_hi[h % 2][:], ALU.subtract).then_inc(sp_lo_done, 1)

        sb_z(0)
        sb_z(1)
        sb_softplus(0)
        sb_lo(0)
        for h in range(SB_HEADS):
            if h + 1 < SB_HEADS:
                sb_softplus(h + 1)
            sb_t(h)
            if h + 1 < SB_HEADS:
                sb_lo(h + 1)
            if h + 2 < SB_HEADS:
                sb_z(h + 2)
            if h >= 2 and h % 2 == 0:
                sb_out(h // 2 - 1)
            if h == 1:
                split_lo(U_OUT[0] + 2)
        sb_out(SB_HEADS // 2 - 1)

        def m_copy(n, u, mp, pair):
            dve.wait_ge(unit_done, u + 1)
            for b in range(2):
                dve.tensor_copy(m[:, 2 * mp + b, :], bank(pair + b)).then_inc(group_evac if b else m_copied, 1)

        def out_projection(layer, n):
            for j in range(N_OUT):
                u = U_OUT[layer] + j
                m_copy(n, u, j, group_banks(group_of(u)))
                if j > 0:
                    split_lo(u + 2)

        def residual(bi, n, which, layer, i):
            dve.scalar_tensor_tensor(out=m[:, i, :], in0=m[:, i, :], scalar=gain(which, layer, i), in1=bank(6),
                                     op0=ALU.mult, op1=ALU.mult).then_inc(post_t, 1)
            dve.wait_ge(post_t, DT * bi + i + 1)
            dve.tensor_tensor(x[:, i, :], x[:, i, :], m[:, i, :], ALU.add).then_inc(x_new, 1)

        def boundary(bi, n, post, pre, u):
            inverse_rms(n)
            dve.wait_ge(bc_mm, n + 1)

            def lo(i):
                dve.wait_ge(hx_hi_done, DT * (bi + 1) + i + 1)
                dve.scalar_tensor_tensor(out=hx_lo[:, i, :], in0=x[:, i, :], scalar=gain(*pre, i), in1=hx_hi[:, i, :],
                                         op0=ALU.mult, op1=ALU.subtract).then_inc(hx_ready, 1)

            for i in range(DT):
                residual(bi, n, *post, i)
                if i:
                    lo(i - 1)
            lo(DT - 1)
            split_lo(u + 2)
            inverse_rms(n + 1)
            spread(n + 1)
            dve.wait_ge(rbc_done, (n + 1) // 2 + 1)

        def ffn_up(layer, j, u, i=None):
            f = FT * layer + j
            g = group_of(u)
            b0 = group_banks(g)
            dve.wait_ge(unit_done, u + 1 if i is None else i * RING + (u + 1))
            if i is not None or j or layer:
                dve.wait_ge(tapped, 4 * f)
            dve.tensor_tensor(ug[:], bank(b0), rbc[:], ALU.mult).then_inc(scaled, 1)
            dve.tensor_tensor(uv[:], bank(b0 + 1), rbc[:], ALU.mult).then_inc(group_evac, 1)
            for s in (1, 2):
                for b, (src, dst) in enumerate(((ug, cg), (uv, cv))):
                    if s == 1:
                        dve.wait_ge(center, 2 * f + b + 1)
                    else:
                        dve.wait_ge(tapped, 4 * f + b + 1)
                    dve.scalar_tensor_tensor(out=dst[:, s:], in0=src[:, 0:T - s], scalar=col(ffn_vec(layer, 2 - s, j + FT * b)),
                                             in1=dst[:, s:], op0=ALU.mult, op1=ALU.add).then_inc(tapped, 1)
            v = split_at(layer, u)
            if v is not None:
                split_lo(v, i=i)
            dve.wait_ge(gelu_done, f + 1)
            dve.wait_ge(tapped, 4 * f + 4)
            dve.tensor_tensor(cv[:], cg[:], cv[:], ALU.mult).then_inc(prod_done, 1)
            dve.wait_ge(g_hi_done, f + 1)
            dve.tensor_tensor(tile_(g_lo, j), cv[:], tile_(g_hi, j), ALU.subtract).then_inc(g_ready, 1)

        def ffn(layer):
            for j in range(3):
                ffn_up(layer, j, U_UP[layer] + j)
            with dve.Fori(0, 5) as i:
                for j in range(RING):
                    ffn_up(layer, i * RING + (3 + j), U_UP[layer] + 3 + j, i)
            for j in range(18, FT):
                ffn_up(layer, j, U_UP[layer] + j)
            for mp in range(4):
                for c in range(3):
                    u = U_DOWN[layer] + 3 * mp + c
                    if c == 2:
                        m_copy(4 * layer + 3, u, mp, group_banks(group_of(u)))
                    v = u + 2
                    if v < U_DOWN[layer] + N_DOWN:
                        k0, k1 = DOWN_K[(3 * mp + c + 2) % 3]
                        split_lo(v, k1 - k0)
                    elif v < N_UNITS:
                        split_lo(v)

        out_projection(0, 1)
        boundary(0, 1, (1, 0), (2, 0), U_UP[0])
        ffn(0)
        boundary(1, 3, (3, 0), (0, 1), U_QKV)

        def rope_finish(i, unit_):
            for b in range(2):
                dve.wait_ge(rope_sw[b], 64 * (i + 1))
                dve.tensor_tensor(rsw[b][:], rsw[b][:], sin_t[:], ALU.mult).then_inc(rope_mul, 1)
                dve.tensor_tensor(rp[b][:], rp[b][:], cos_t[:], ALU.mult).then_inc(rope_mul, 1)
            for b in range(2):
                dve.wait_ge(rope_mul, 4 * i + 2 * b + 2)
                if unit_ == "k":
                    for h in range(2):
                        hh = slice(HD * h, HD * h + HD)
                        dve.tensor_tensor(kr[hh, 2 * b + h, :], rp[b][hh, :], rsw[b][hh, :], ALU.add).then_inc(rope_done, 1)
                else:
                    chunks = [t[b][:].rearrange("p (c t) -> p c t", t=CHUNK) for t in (rp, rsw)]
                    dve.tensor_tensor(qr[:, unit_, :, b, :], chunks[0], chunks[1], ALU.add).then_inc(rope_done, 1)

        pairs = {0: (0, "k"), 1: (1, 0), 2: (2, 1), 3: (3, 2), 4: (4, 3)}
        last = None
        for k in range(N_QKV):
            u = U_QKV + k
            b0 = group_banks(group_of(u))
            if last is not None:
                rope_finish(*last)
                last = None
            dve.wait_ge(unit_done, u + 1)
            if k == N_QKV - 1:
                for t in range(TT):
                    c = T * b0 + 256 * t
                    dve.tensor_scalar(v1[:, t, :], ps[:, c:c + 256], rcol[:, t:t + 1], None, ALU.mult).then_inc(v_raw if t < TT - 1 else group_evac, 1)
                dve.wait_ge(group_evac, group_of(u) + 1)
                dve.tensor_copy(narrow[:, 8, 0:1], rcol[:, 0:1]).then_inc(v_raw, 1)
            else:
                i, dst = pairs[k]
                dve.wait_ge(rope_done, 2 * i + 2) if i else None
                for b in range(2):
                    if k == 0:
                        dve.tensor_tensor(rp[b][:], bank(b0 + b), rbc[:], ALU.mult).then_inc(rope_raw, 1)
                    else:
                        dve.scalar_tensor_tensor(out=rp[b][:], in0=bank(b0 + b), scalar=SCALE, in1=rbc[:], op0=ALU.mult, op1=ALU.mult).then_inc(rope_raw, 1)
                dve.wait_ge(rope_raw, 2 * i + 2)
                dve.tensor_copy(narrow[:, 8, 0:1], rcol[:, 0:1]).then_inc(group_evac, 1)
                last = pairs[k]
            if k != 2:
                split_lo(u + (3 if k < 2 else 2))

        def sw_max(c):
            kw = HD if c == 0 else P
            o = 4 * (c % 2)
            dve.wait_ge(s_mm, c + 1)
            bk = bank(2 * (c % 2), 2).rearrange("p (e k) -> p e k", k=P)
            if c >= 2:
                dve.wait_ge(ex_done, c - 1)
            dve.tensor_reduce(narrow[:, o, 0:8], bk[:, :, 0:kw], AX.X, ALU.max).then_inc(smax_done, 1)
            dve.wait_ge(smax_done, c + 1)
            dve.tensor_tensor(narrow[:, o, 0:8], narrow[:, o, 0:8], sink[:], ALU.max).then_inc(sw_step, 1)
            dve.wait_ge(sw_step, 4 * c + 1)
            dve.tensor_tensor(narrow[:, o + 3, 0:8], sink[:], narrow[:, o, 0:8], ALU.subtract).then_inc(sw_step, 1)
            dve.tensor_scalar(narrow[:, o, 0:8], narrow[:, o, 0:8], -1.0, None, ALU.mult).then_inc(negm_done, 1)

        def sw_norm(c):
            kw = HD if c == 0 else P
            o = 4 * (c % 2)
            dve.wait_ge(ex_done, c + 1)
            dve.tensor_tensor(narrow[:, o + 1, 0:8], narrow[:, o + 1, 0:8], narrow[:, o + 2, 0:8], ALU.add).then_inc(sw_step, 1)
            dve.wait_ge(sw_step, 4 * c + 3)
            dve.reciprocal(narrow[:, o + 1, 0:8], narrow[:, o + 1, 0:8]).then_inc(sw_step, 1)
            dve.wait_ge(sw_step, 4 * c + 4)
            pr = prob[c % 2][:, :, 0:kw]
            dve.tensor_tensor(pr, pr, narrow[:, o + 1, 0:8].unsqueeze(2).broadcast_to([P, 8, kw]), ALU.mult).then_inc(pn_done, 1)

        def sw_lo(c):
            dve.wait_ge(y_hi_done, 1 + LT + c + 1)
            ys = slice(CHUNK * c, CHUNK * c + CHUNK)
            dve.tensor_tensor(y_lo[:, :, ys], bank(6).rearrange("p (k t) -> p k t", t=CHUNK), y_hi[:, :, ys], ALU.subtract).then_inc(y_ready, 1)

        sw_max(0)
        for c in range(NCH):
            sw_norm(c)
            if c + 1 < NCH:
                sw_max(c + 1)
            if c == 1:
                split_lo(U_OUT[1] + 2)
            if c >= 1:
                sw_lo(c - 1)
        sw_lo(NCH - 1)

        out_projection(1, 5)
        boundary(2, 5, (1, 1), (2, 1), U_UP[1])
        ffn(1)
        inverse_rms(7)
        dve.wait_ge(bc_mm, 8)
        for i in range(DT):
            residual(3, 7, 3, 1, i)
            if i:
                o = i - 1
                dve.wait_ge(out_mm, o + 1)
                dve.tensor_copy(out_s[:, :, P * o:P * o + P], bank(o % 4).rearrange("p (t c) -> p t c", c=P)).then_inc(out_copied, 1)
        o = DT - 1
        dve.wait_ge(out_mm, o + 1)
        dve.tensor_copy(out_s[:, :, P * o:P * o + P], bank(o % 4).rearrange("p (t c) -> p t c", c=P)).then_inc(out_copied, 1)

    @block.tensor
    def _(pe):
        def three(dst, s_hi, s_lo, r_hi, r_lo, first, last):
            pe.matmul(dst, s_hi, r_hi, start=first, stop=False)
            pe.matmul(dst, s_hi, r_lo, start=False, stop=False)
            return pe.matmul(dst, s_lo, r_hi, start=False, stop=last)

        def unit_ready(u, i=None):
            pe.wait_ge(w_lo_done, u + 1 if i is None else i * RING + (u + 1))

        def banks_free(g, i=None):
            if i is not None:
                pe.wait_ge(group_evac, i * RING + (g - 2))
            elif g >= 3:
                pe.wait_ge(group_evac, g - 2)

        def weights(u, k, b):
            s = u % RING
            return w_hi[s][:, k, b, :], w_lo[s][:, k, b, :]

        def columns(u, ks, src, b0, k_first=0, k_last=UK - 1, koff=0):
            for b in range(2):
                for k in ks:
                    last = three(bank(b0 + b), *weights(u, k, b), src[0][:, k + koff, :], src[1][:, k + koff, :],
                                 k + koff == k_first, k + koff == k_last)
            return last

        def tokens(u, b0):
            s = u % RING
            for t in range(TT):
                dst = ps[:, T * b0 + 256 * t:T * b0 + 256 * t + 256]
                tt = slice(P * t, P * t + P)
                for k in range(UK):
                    r = [w[s][:, k].rearrange("p b n -> p (b n)") for w in (w_hi, w_lo)]
                    last = three(dst, hx_hi[:, k, tt], hx_lo[:, k, tt], r[0], r[1], k == 0, k == UK - 1)
            return last

        hx = (hx_hi, hx_lo)
        y = (y_hi, y_lo)
        gg = (g_hi, g_lo)

        def mean_square(n):
            if n:
                pe.wait_ge(std_done, n)
            pe.wait_ge(sum_done, N_SUMS * (n + 1))
            pe.wait_ge(sq_done, DT * (n + 1))
            for t in range(TT):
                for src in (sumsq, *sq):
                    last = pe.matmul(bank(7)[:, t:t + 1], src[:, P * t:P * t + P], ones[:, 0:1], start=src is sumsq, stop=src is sq[1])
            last.then_inc(ms_mm, 1)

        def spread(n):
            pe.wait_ge(diag_done, n + 1)
            pe.matmul(bank(6), ones, diag[:].rearrange("p t c -> p (t c)"), start=True, stop=True).then_inc(bc_mm, 1)

        def first_two(u, ready, fill=None):
            for j in range(2):
                banks_free(group_of(u + j))
                unit_ready(u + j)
            for k in range(UK):
                ready(k)
                if fill is not None:
                    fill(k)
                for j in range(2):
                    b0 = group_banks(group_of(u + j))
                    src = y if u in U_OUT else hx
                    last = None
                    for b in range(2):
                        last = three(bank(b0 + b), *weights(u + j, k, b), src[0][:, k, :], src[1][:, k, :], k == 0, k == UK - 1)
                    if k == UK - 1:
                        last.then_inc(unit_done, 1)

        def unit(u, src, i=None):
            g = group_of(u)
            banks_free(g, i)
            unit_ready(u, i)
            columns(u, range(UK), src, group_banks(g)).then_inc(unit_done, 1)

        pe.wait_ge(const_in, 16)
        pe.wait_ge(vec_in, 16 * 15)
        c = 0
        for r, n in enumerate([V_ROWS0] + [4 * FT] * 4):
            last = pe.transpose(bank(5)[:, c:c + n], vrow[0:n, r, :], ident[0:n, 0:n])
            c += n
        last.then_inc(vec_mm, 1)

        def turn(i):
            pe.wait_ge(x_loaded[i // 2], 16)
            if i >= 2:
                pe.wait_ge(xt_copied, i - 1)
            for t in range(TT):
                last = pe.transpose(bank(6 + i % 2)[:, P * t:P * t + P], x_in[:, t, P * i:P * i + P], ident)
            last.then_inc(xt_mm, 1)

        turn(0)
        turn(1)
        def fill_start(k):
            if k + 2 < DT:
                turn(k + 2)
            if k == DT - 1:
                pe.wait_ge(xt_copied, DT)
                mean_square(0)

        first_two(U_IN, lambda k: pe.wait_ge(hx_ready, k + 1), fill=fill_start)
        spread(0)
        pe.wait_ge(vec_done, 1)
        pe.wait_ge(gates_in, 64)
        for u in range(2, N_IN):
            if u < 8:
                unit(u, hx)
            else:
                banks_free(group_of(u))
                unit_ready(u)
                tokens(u, group_banks(group_of(u))).then_inc(unit_done, 1)
            if 2 <= u < 6:
                t = u - 2
                if t == 0:
                    pe.wait_ge(rbc_done, 1)
                    pe.wait_ge(std_done, 1)
                pe.wait_ge(xc_tap, 6 * (t // 2 + 1))
                for b in range(2):
                    if t:
                        pe.wait_ge(gate_act, 2 * t - 1 + b)
                    pe.matmul(bank(6 + b), gate_w[:, b, t, :], xc[:, t, :], start=True, stop=True).then_inc(gate_mm, 1)

        def sb_z(h):
            hh = slice(HD * (h % 2), HD * (h % 2) + HD)
            if h:
                pe.wait_ge(z_copied, h)
            for j in range(TT):
                dst = ps[:, OFF[j]:OFF[j] + T - P * j]
                pe.matmul(dst, kT[hh, h // 2, P * j:P * j + P], qT[hh, h // 2, P * j:T], start=True, stop=False)
                last = pe.matmul(dst[:, 0:P], ident_b[:], mask_b[:], start=False, stop=True)
            last.then_inc(z_mm, 1)

        def sb_cum(h):
            pe.wait_ge(sp_lo_done, h + 1)
            if h:
                pe.wait_ge(t_done, h)
            for j in range(TT):
                for jj in range(j, TT):
                    n = T - P * jj
                    dst = ps[:, 3 * T + OFF[j] + P * (jj - j):3 * T + OFF[j] + P * (jj - j) + n]
                    for part in (sp_hi[h % 2], sp_lo[h % 2]):
                        last = pe.matmul(dst, (tri_r if jj == j else ones_r)[:], part[:, OFF[jj]:OFF[jj] + n],
                                         start=(jj == j and part is sp_hi[h % 2]), stop=(jj == TT - 1 and part is not sp_hi[h % 2]))
            last.then_inc(cum_mm, 1)

        def sb_av(h):
            ti, hh = h // 2, h % 2
            pe.wait_ge(w_done, h + 1)
            if ti >= 2 and hh == 0:
                pe.wait_ge(y_ready, 1 + ti - 1)
            for j in range(TT):
                n = T - P * j
                last = pe.matmul(bank(6 + ti % 2)[HD * hh:HD * hh + HD, P * j:T], v0[:, j, HD * h:HD * h + HD],
                                 z_s[h % 3][:, OFF[j]:OFF[j] + n], start=(j == 0), stop=(j == TT - 1))
            last.then_inc(av_mm, 1)

        pe.wait_ge(group_evac, N_IN)
        pe.wait_ge(consts_cast, 1)
        sb_z(0)
        sb_z(1)
        pe.wait_ge(gate_act, 2 * LT)
        for h in range(SB_HEADS):
            sb_cum(h)
            if h + 2 < SB_HEADS:
                sb_z(h + 2)
            sb_av(h)

        def boundary(n, bi, u):
            mean_square(n)
            spread(n)
            first_two(u, lambda k: pe.wait_ge(hx_ready, DT * (bi + 1) + k + 1),
                      fill=lambda k: mean_square(n + 1) if k == DT - 1 else None)
            spread(n + 1)

        def out_projection(layer):
            first_two(U_OUT[layer], (lambda k: pe.wait_ge(y_ready, 1 if k < LT else k - LT + 2)) if layer == 0 else
                      (lambda k: pe.wait_ge(y_ready, 1 + LT + NCH)))
            for j in range(2, N_OUT):
                unit(U_OUT[layer] + j, y)

        def ffn(layer, bi):
            u0 = U_UP[layer]
            n = 4 * layer + 1
            boundary(n, bi, u0)
            for j in range(2, 5):
                unit(u0 + j, hx)
            with pe.Fori(1, 6) as i:
                for j in range(RING):
                    unit(u0 + 2 + j, hx, i=i)
            for j in range(20, FT):
                unit(u0 + j, hx)
            g_up = group_of(U_DOWN[layer])
            for mp in range(4):
                b0 = group_banks(g_up + mp)
                banks_free(g_up + mp)
                for c, (k0, k1) in enumerate(DOWN_K):
                    u = U_DOWN[layer] + 3 * mp + c
                    unit_ready(u)
                    pe.wait_ge(g_ready, FT * layer + k1)
                    columns(u, range(k1 - k0), gg, b0, k_last=FT - 1, koff=k0).then_inc(unit_done, 1)

        out_projection(0)
        ffn(0, 0)
        boundary(3, 1, U_QKV)
        for k in range(2, N_QKV):
            u = U_QKV + k
            if k == N_QKV - 1:
                banks_free(group_of(u))
                unit_ready(u)
                tokens(u, group_banks(group_of(u))).then_inc(unit_done, 1)
            else:
                unit(u, hx)

        def sw_scores(c):
            if c >= 2:
                pe.wait_ge(ex_done, c - 1)
            kw = HD if c == 0 else P
            k0 = 0 if c == 0 else CHUNK * (c - 1)
            for e in range(8):
                kv, hh = e % KV, slice(HD * (e // KV), HD * (e // KV) + HD)
                dst = ps[:, T * 2 * (c % 2) + P * e:T * 2 * (c % 2) + P * e + kw]
                last = pe.matmul(dst, qr[hh, kv, c].rearrange("p g t -> p (g t)"), kr[hh, kv, k0:k0 + kw], start=True, stop=True)
            last.then_inc(s_mm, 1)

        def sw_turn(c):
            kw = HD if c == 0 else P
            pe.wait_ge(pn_done, c + 1)
            if c:
                pe.wait_ge(pt_copied, 2 * c)
            for e in range(8):
                last = pe.transpose(ps[0:kw, T * 4 + P * e:T * 4 + P * e + P], prob[c % 2][:, e, 0:kw], ident)
                if e % 4 == 3:
                    last.then_inc(pt_mm, 1)

        def sw_values(c):
            pe.wait_ge(pt_copied, 2 * (c + 1))
            if c:
                pe.wait_ge(y_ready, 1 + LT + c)
            kw = HD if c == 0 else P
            v = v1[0:HD, 0] if c == 0 else (v1[:, (c - 1) // 2] if c % 2 else v1s[:, c // 2])
            for e in range(8):
                kv, h = e % KV, e // KV
                dst = bank(6)[HD * h:HD * h + HD, P * kv:P * kv + P]
                last = pe.matmul(dst, v[:, HD * kv:HD * kv + HD], probT[c % 2][0:kw, e, :], start=True, stop=True)
            last.then_inc(o_mm, 1)

        pe.wait_ge(group_evac, group_of(U_QKV + N_QKV))
        pe.wait_ge(rope_done, 12)
        pe.wait_ge(k_copied, 64)
        pe.wait_ge(v_shift, 32)
        sw_scores(0)
        sw_scores(1)
        for c in range(NCH):
            sw_turn(c)
            if c + 2 < NCH:
                sw_scores(c + 2)
            sw_values(c)

        out_projection(1)
        ffn(1, 2)
        mean_square(7)
        spread(7)
        for i in range(DT):
            pe.wait_ge(x_new, 3 * DT + i + 1)
            if i >= 4:
                pe.wait_ge(out_copied, i - 3)
            for t in range(TT):
                last = pe.transpose(bank(i % 4)[:, P * t:P * t + P], x[:, i, P * t:P * t + P], ident)
            last.then_inc(out_mm, 1)

    es.close()


_INS = ["x", "positions", "even_w_in", "even_conv_w", "even_conv_b", "lru_w_a", "lru_b_a", "lru_w_x", "lru_b_x",
        "lru_lambda", "even_w_out", "odd_w_qkv", "odd_sinks", "odd_w_o", "ffn_w_up", "ffn_conv_w", "ffn_conv_b",
        "ffn_w_down", "norm_mix_pre", "norm_mix_post", "norm_ffn_pre", "norm_ffn_post"]


def _consts():
    c = np.zeros((P, 4 * P + 2), np.float32)
    s, t = np.arange(P)[:, None], np.arange(P)[None, :]
    c[:, 0:P] = s == t
    c[:, P:2 * P] = 1.0
    c[:, 2 * P:3 * P] = s >= t
    c[:, 3 * P:4 * P] = np.where(s >= t, MASKED, 0.0)
    half = HD // 2
    c[:, 4 * P] = (10000.0 ** (-np.arange(half) / half)).astype(np.float32)[np.arange(P) % half]
    c[:, 4 * P + 1] = np.where(np.arange(P) % HD < half, -1.0, 1.0)
    return c


def kernel(**inputs):
    import concourse.bacc as bacc
    from concourse.bass_utils import run_bass_kernel_spmd

    nc = bacc.Bacc("TRN2", target_bir_lowering=False, num_devices=1)
    arrays, io = {}, {}
    for name in _INS + ["consts"]:
        a = _consts() if name == "consts" else np.ascontiguousarray(inputs[name])
        arrays[f"in_{name}"] = a
        io[name] = nc.dram_tensor(f"in_{name}", a.shape, mybir.dt.from_np(a.dtype), kind="ExternalInput").ap()
    out = nc.dram_tensor("out", (1, T, D), F32, kind="ExternalOutput").ap()
    build(nc, io, out)
    r = run_bass_kernel_spmd(nc, [arrays], core_ids=[0])
    return r.results[0]["out"]
```

```python
from contextlib import ExitStack

import numpy as np
import concourse.bass as bass
from concourse import mybir

F32 = mybir.dt.float32
F32R = mybir.dt.float32r
BF16 = mybir.dt.bfloat16
I32 = mybir.dt.int32
ALU = mybir.AluOpType
ACT = mybir.ActivationFunctionType
AX = mybir.AxisListType

P = 128
T = 512
D = 1024
DT = D // P
TT = T // P
LRU = 512
LT = LRU // P
HD = 64
SB_HEADS = 8
F = 2816
FT = F // P
CHUNK = 64
NCH = T // CHUNK
KV = 4
EPS = 1e-6
SCALE = HD ** -0.5
MASKED = -1e30

RING = 3
UK = 8
DOWN_K = [(0, 8), (8, 16), (16, FT)]
N_IN, N_OUT, N_UP, N_DOWN, N_QKV = 10, 4, FT, 4 * len(DOWN_K), 6
U_IN = 0
U_OUT = [N_IN, 0]
U_UP = [U_OUT[0] + N_OUT, 0]
U_DOWN = [U_UP[0] + N_UP, 0]
U_QKV = U_DOWN[0] + N_DOWN
U_OUT[1] = U_QKV + N_QKV
U_UP[1] = U_OUT[1] + N_OUT
U_DOWN[1] = U_UP[1] + N_UP
N_UNITS = U_DOWN[1] + N_DOWN
G_SHIFT = N_DOWN - 4
N_SUMS = DT - 3

V_CONV = 64
V_CONVB, V_BA, V_BX, V_LAM = V_CONV + 16, V_CONV + 20, V_CONV + 24, V_CONV + 28
V_ROWS0 = V_LAM + 4
V_ROWSF = 4 * 2 * FT


def group_of(u):
    shift = 0
    for layer in range(2):
        if u >= U_DOWN[layer] + N_DOWN:
            shift += G_SHIFT
        elif u >= U_DOWN[layer]:
            return U_DOWN[layer] - shift + (u - U_DOWN[layer]) // len(DOWN_K)
    return u - shift


G_QKV = group_of(U_QKV)


def evacuated(g):
    return g + 1 if g < G_QKV else g + 1 - N_QKV


def dmas_of(u):
    for layer in range(2):
        if U_UP[layer] <= u < U_DOWN[layer]:
            return 2
    return 1


def loaded_at(u):
    return 16 * sum(dmas_of(v) for v in range(u % RING, u + 1, RING) if v >= 2)


def build(nc, io, out):
    es = ExitStack()
    sem_names = {}

    def sem(name):
        sem_names[name] = es.enter_context(nc.semaphore(name))
        return sem_names[name]

    base = (nc.sbuf_base + 31) // 32 * 32
    where = [base]

    def at(name, shape, dt, offset):
        return nc.alloc_sbuf_tensor_at(name, shape, dt, offset=offset)

    def size(shape, dt):
        n = 2 if dt == BF16 else 4
        for s in shape[1:]:
            n *= s
        return (n + 31) // 32 * 32

    def place(name, shape, dt):
        t = at(name, shape, dt, where[0])
        where[0] += size(shape, dt)
        return t

    w_raw, w_lo, w_hi = [], [], []
    for s in range(RING):
        w_lo.append(at(f"w_lo{s}", [P, UK, 2, P], F32R, where[0]))
        w_raw.append(place(f"w_raw{s}", [P, UK, 2, P], F32))
        w_hi.append(place(f"w_hi{s}", [P, UK, 2, P], F32R))
    x = place("x", [P, DT, T], F32)
    m_at = where[0]
    m = at("m", [P, DT, T], F32, m_at)
    hx_hi = place("hx_hi", [P, DT, T], F32R)
    hx_lo = place("hx_lo", [P, DT, T], F32R)
    const = place("const", [P, 4 * P + 2], F32)
    ident, ones, tri, mask = (const[:, P * i:P * i + P] for i in range(4))
    inv_freq, rope_sign = const[:, 4 * P:4 * P + 1], const[:, 4 * P + 1:4 * P + 2]
    tri_r = place("tri_r", [P, P], F32R)
    ones_r = place("ones_r", [P, P], F32R)
    ident_b = place("ident_b", [P, P], BF16)
    mask_b = place("mask_b", [P, P], BF16)
    vec = place("vec", [P, V_ROWS0 + 2 * V_ROWSF], F32)
    nlam = place("nlam", [P, LT], F32)
    plam = place("plam", [P, LT], F32)
    narrow = place("narrow", [P, 10, 8], F32)
    std = place("std", [P, TT], F32)
    rcol = place("rcol", [P, TT], F32)
    sink = place("sink", [P, 8], F32)
    sink_row = place("sink_row", [P, 16], F32)
    rbc = place("rbc", [P, T], F32)
    tables_at = where[0]
    cos_t = place("cos_t", [P, T], F32)
    sin_t = place("sin_t", [P, T], F32)
    sumsq_at = where[0]
    sumsq = place("sumsq", [P, T], F32)
    tmp0 = where[0]
    ug = place("ug", [P, T], F32)
    uv = place("uv", [P, T], F32)
    cg = place("cg", [P, T], F32)
    cv = place("cv", [P, T], F32)
    big0 = where[0]
    g_hi = place("g_hi", [P, FT, T], F32R)
    g_lo = place("g_lo", [P, FT, T], F32R)
    assert where[0] <= nc.sbuf_usable_end, (where[0], nc.sbuf_usable_end)
    sq = [at(f"sq{b}", [P, T], F32, tmp0 + 2 * b * T * 4) for b in range(2)]
    diag = at("diag", [P, TT, P], F32, tmp0 + T * 4)

    class big:
        at_ = big0

    def inbig(name, shape, dt):
        t = at(name, shape, dt, big.at_)
        big.at_ += size(shape, dt)
        assert big.at_ <= where[0], name
        return t

    x_in = inbig("x_in", [P, TT, D], F32)
    vrow = inbig("vrow", [P, 5, P], F32)
    pos_i = inbig("pos_i", [P, T], I32)
    ang = inbig("ang", [P, T], F32)
    turns = inbig("turns", [P, T], F32)
    angc = inbig("angc", [P, T], F32)
    start_end = big.at_
    gate_w = at("gate_w", [P, 2, LT, P], F32, start_end)
    big.at_ = big0
    y_hi = inbig("y_hi", [P, DT, T], F32R)
    y_lo = inbig("y_lo", [P, DT, T], F32R)
    mix0 = big.at_
    assert start_end + 2 * LT * P * 4 <= mix0
    lru_a = at("lru_a", [P, LT, T], F32, big0 + LT * T * 4)
    lru_th = at("lru_th", [P, LT, T], F32, big0 + (DT + LT) * T * 4)
    qT = inbig("qT", [P, LT, T], F32)
    kT = inbig("kT", [P, LT, T], F32)
    v0 = inbig("v0", [P, TT, LRU], F32)
    att0 = big.at_
    xc = inbig("xc", [P, LT, T], F32)
    gr = inbig("gr", [P, LT, T], F32)
    lru_r = inbig("lru_r", [P, LT, T], F32)
    lru_i = inbig("lru_i", [P, LT, T], F32)
    big.at_ = att0
    SPAN = sum(T - P * j for j in range(TT))
    OFF = [0, T, 2 * T, T + (T - P)]
    z_s = [inbig(f"z_s{b}", [P, SPAN], F32) for b in range(4)]
    sp_lo = [at(f"sp_lo{b}", [P, SPAN], F32R, big.at_ + b * SPAN * 4) for b in range(2)]
    sp = [inbig(f"sp{b}", [P, SPAN], F32) for b in range(2)]
    assert sumsq_at + 2 * SPAN * 4 <= big0
    sp_hi = [at(f"sp_hi{b}", [P, SPAN], F32R, sumsq_at + b * SPAN * 4) for b in range(2)]
    big.at_ = mix0
    qr = inbig("qr", [P, KV, NCH, 2, CHUNK], F32)
    kz = [inbig("kz0", [P, KV, T], F32), at("kz1", [P, KV, T], F32, tmp0)]
    assert tmp0 + KV * T * 4 <= big0
    v1 = inbig("v1", [P, TT, KV * HD], F32)
    v1s = inbig("v1s", [P, TT, KV * HD], F32)
    rp = [[inbig(f"rp0{b}", [P, T], F32) for b in range(2)]]
    rsw = [[inbig(f"rsw0{b}", [P, T], F32) for b in range(2)]]
    rp.append([at(f"rp1{b}", [P, T], F32, big.at_ + b * T * 4) for b in range(2)])
    rsw.append([at(f"rsw1{b}", [P, T], F32, big.at_ + (2 + b) * T * 4) for b in range(2)])
    prob = [inbig(f"prob{b}", [P, 8, P], F32) for b in range(2)]
    probT = [inbig(f"probT{b}", [P, 8, P], F32) for b in range(2)]
    m_tok = at("m_tok", [P, TT, D], F32, m_at)
    x_tok = at("x_tok", [P, TT, D], F32, m_at + TT * D * 4)
    last_gain = at("last_gain", [P, D], F32, tables_at)

    ps = es.enter_context(nc.psum_tensor("ps", [P, 8 * T], F32))

    def bank(b, n=1):
        return ps[:, T * b:T * (b + n)]

    def group_banks(g):
        return 6 if g == N_IN - 1 else 2 * (g % 3)

    const_in, vec_in, pos_in, gates_in, sink_in = (sem(n) for n in (
        "const_in", "vec_in", "pos_in", "gates_in", "sink_in"))
    x_loaded = [sem(f"x_loaded{q}") for q in range(4)]
    first_in = [sem(f"first_in{n}") for n in range(8)]
    first_hi, first_lo, pregain_in = sem("first_hi"), sem("first_lo"), sem("pregain_in")
    w_loaded = [sem(f"w_loaded{s}") for s in range(RING)]
    w_hi_done, w_lo_done, unit_done, group_evac = (sem(n) for n in (
        "w_hi_done", "w_lo_done", "unit_done", "group_evac"))
    zeroed, consts_cast, vec_mm, vec_done, xt_mm, xt_copied = (sem(n) for n in (
        "zeroed", "consts_cast", "vec_mm", "vec_done", "xt_mm", "xt_copied"))
    hx_hi_done, hx_ready, post_t, x_new, m_first = (sem(n) for n in (
        "hx_hi_done", "hx_ready", "post_t", "x_new", "m_first"))
    sq_done, sum_done, ms_mm, std_done, rcol_done, diag_done, bc_mm, rbc_done = (sem(n) for n in (
        "sq_done", "sum_done", "ms_mm", "std_done", "rcol_done", "diag_done", "bc_mm", "rbc_done"))
    setup_v, setup_a = sem("setup_v"), sem("setup_a")
    xc_center, xc_tap, gate_mm, gate_act, lru_act, lru_dve = (sem(n) for n in (
        "xc_center", "xc_tap", "gate_mm", "gate_act", "lru_act", "lru_dve"))
    y_hi_done, y_ready = sem("y_hi_done"), sem("y_ready")
    z_mm, z_copied, abs_done, exp_done, ln_done, sp_done, sp_hi_done, sp_lo_done = (sem(n) for n in (
        "z_mm", "z_copied", "abs_done", "exp_done", "ln_done", "sp_done", "sp_hi_done", "sp_lo_done"))
    cum_mm, t_done, w_done, av_mm = (sem(n) for n in ("cum_mm", "t_done", "w_done", "av_mm"))
    scaled, center, tapped, gelu_done, prod_done, g_hi_done, g_ready = (sem(n) for n in (
        "scaled", "center", "tapped", "gelu_done", "prod_done", "g_hi_done", "g_ready"))
    rope_sw = [[sem(f"rope_swapped{i}{b}") for b in range(2)] for i in range(2)]
    rope_raw, rope_mul, rope_done, v_shift, v_raw = (sem(n) for n in (
        "rope_raw", "rope_mul", "rope_done", "v_shift", "v_raw"))
    k_copied, kz_zeroed = sem("k_copied"), sem("kz_zeroed")
    s_mm, smax_done, negm_done, p_done, ex_done, sw_step, pn_done, pt_mm, pt_copied, o_mm = (sem(n) for n in (
        "s_mm", "smax_done", "negm_done", "p_done", "ex_done", "sw_step", "pn_done", "pt_mm", "pt_copied", "o_mm"))
    last_gain_in, xtok_mm, xtok_copied, mtok_mm, mtok_sq, mtok_done = (sem(n) for n in (
        "last_gain_in", "xtok_mm", "xtok_copied", "mtok_mm", "mtok_sq", "mtok_done"))
    tok_sum, tok_std, tok_rms, out_done, stored = (sem(n) for n in ("tok_sum", "tok_std", "tok_rms", "out_done", "stored"))

    PHASES = [U_IN, U_OUT[0], U_UP[0], U_DOWN[0], U_QKV, U_OUT[1], U_UP[1], U_DOWN[1]]
    FFN_TAPS = V_ROWS0

    def ffn_vec(layer, what, j):
        return FFN_TAPS + V_ROWSF * layer + 2 * FT * what + j

    def gain(which, layer, i):
        c = 16 * which + 8 * layer + i
        return vec[:, c:c + 1]

    def col(c):
        return vec[:, bass.ds(c, 1)] if not isinstance(c, int) else vec[:, c:c + 1]

    def tile_(t, i):
        return t[:, bass.ds(i, 1), :].rearrange("p a t -> p (a t)") if not isinstance(i, int) else t[:, i, :]

    def sw_banks(c):
        return 2 * (1 - c % 2)

    def split_at(layer, u):
        return {0: u + 3, 1: u + 3, 2: None}.get(u - U_UP[layer], u + 2)

    block = es.enter_context(nc.Block())

    def first_piece(n):
        return n % 2, slice(2 * (n // 2), 2 * (n // 2) + 2)

    def piece_signal(n, early, done):
        return done if n >= 6 else early

    def piece_wait(engine, n, early, done):
        if n >= 6:
            engine.wait_ge(done, n - 5)
        else:
            engine.wait_ge(early, n + 1)

    def swap_halves(queue, i, b):
        queue.wait_ge(rope_raw, 2 * i + b + 1)
        for a in range(4):
            c = a ^ 1
            queue.dma_start(rsw[i % 2][b][32 * a:32 * a + 32, :], rp[i % 2][b][32 * c:32 * c + 32, :]).then_inc(rope_sw[i % 2][b], 16)

    @block.sync
    def _(sp_):
        def slot_free(u, i=None, per=0):
            if i is not None:
                sp_.wait_ge(unit_done, i * per + (u - RING + 1))
            elif u >= RING:
                sp_.wait_ge(unit_done, u - RING + 1)

        def load(u, src, dst=None):
            s = u % RING
            sp_.dma_start(w_raw[s][:] if dst is None else dst, src).then_inc(w_loaded[s], 16)

        def cols(w, c0, n=2 * P):
            c = slice(c0, c0 + n) if isinstance(c0, int) else bass.ds(c0, n)
            return w[:, c].rearrange("(k p) n -> p k n", p=P)

        def whole(s, k=UK):
            return w_raw[s][:, 0:k].rearrange("p k b n -> p k (b n)")

        def load_cols(u, w, c0):
            slot_free(u)
            load(u, cols(w, c0), whole(u % RING))

        w_in, w_qkv = io["even_w_in"][0], io["odd_w_qkv"][0]
        order = [0, 256, 512, 768, 1024, 1280, 1536, 1792, 2048, 2304]
        sp_.dma_start(const[:], io["consts"]).then_inc(const_in, 16)
        xv = io["x"][0].rearrange("(t p) d -> p t d", p=P)
        for q in range(4):
            sp_.dma_start(x_in[:, :, 256 * q:256 * q + 256], xv[:, :, 256 * q:256 * q + 256]).then_inc(x_loaded[q], 16)
            if q == 0:
                sp_.dma_start(vrow[0:16, 0, :], io["norm_mix_pre"].rearrange("l (i c) -> (l i) c", c=P)).then_inc(pregain_in, 16)
            for n in (2 * q, 2 * q + 1):
                u, ks = first_piece(n)
                sp_.dma_start(w_raw[u][:, ks].rearrange("p k b n -> p k (b n)"),
                              cols(w_in, order[u])[:, ks]).then_inc(first_in[n], 16)
        row = 16
        rows = [(io[n].rearrange("l (i c) -> (l i) c", c=P), 16) for n in ("norm_mix_post", "norm_ffn_pre", "norm_ffn_post")]
        rows.append((io["even_conv_w"][0].rearrange("k (i c) -> (k i) c", c=P), 16))
        rows.append((io["even_conv_b"][0].rearrange("(i c) -> i c", c=P), 4))
        rows.append((io["lru_b_a"][0].rearrange("(i a) c -> i (a c)", a=2), 4))
        rows.append((io["lru_b_x"][0].rearrange("(i a) c -> i (a c)", a=2), 4))
        rows.append((io["lru_lambda"][0].rearrange("(i c) -> i c", c=P), 4))
        for src, n in rows:
            sp_.dma_start(vrow[row:row + n, 0, :], src).then_inc(vec_in, 16)
            row += n
        for layer in range(2):
            wv = io["ffn_conv_w"][layer].rearrange("k (i c) -> (k i) c", c=P)
            bv = io["ffn_conv_b"][layer].rearrange("(i c) -> i c", c=P)
            n = 2 * FT
            sp_.dma_start(vrow[0:2 * n, 1 + 2 * layer, :], wv[0:2 * n]).then_inc(vec_in, 16)
            sp_.dma_start(vrow[0:n, 2 + 2 * layer, :], wv[2 * n:3 * n]).then_inc(vec_in, 16)
            sp_.dma_start(vrow[n:2 * n, 2 + 2 * layer, :], bv).then_inc(vec_in, 16)
        load_cols(2, w_in, order[2])
        sp_.dma_start(pos_i[:], io["positions"][0:1, :].broadcast_to([P, T])).then_inc(pos_in, 16)
        sp_.dma_start(sink_row[:], io["odd_sinks"][0:1, :].broadcast_to([P, 16])).then_inc(sink_in, 16)
        sp_.wait_ge(zeroed, 1)
        for g, name in enumerate(("lru_w_a", "lru_w_x")):
            wv = io[name][0].rearrange("(i a) c d -> a c i d", a=2)
            for a in range(2):
                sp_.dma_start(gate_w[64 * a:64 * a + 64, g, :, 64 * a:64 * a + 64], wv[a]).then_inc(gates_in, 16)
        for u in range(3, N_IN):
            load_cols(u, w_in, order[u])

        for layer in range(2):
            if layer == 1:
                for j, c0 in enumerate((D, 0, 256)):
                    load_cols(U_QKV + j, w_qkv, c0)

                def swap(i):
                    swap_halves(sp_, i, 0)

                load_cols(U_QKV + 3, w_qkv, 512)
                load_cols(U_QKV + 4, w_qkv, 768)
                swap(0)
                swap(1)
                load_cols(U_QKV + 5, w_qkv, D + KV * HD)
                swap(2)
                sp_.wait_ge(rope_done, 4)
                for kv in range(KV):
                    a, b = kv % 2, 1 - kv % 2
                    sp_.dma_start(kz[b][HD * b:HD * b + HD, kv, :], kz[a][HD * a:HD * a + HD, kv, :]).then_inc(k_copied, 16)
                for i in range(3, 5):
                    load_cols(U_OUT[layer] + i - 3, io["odd_w_o"][0], 256 * (i - 3))
                    swap(i)
                sp_.wait_ge(v_raw, 4)
                sp_.dma_start(v1s[0:64, 1:TT, :], v1[64:128, 0:TT - 1, :]).then_inc(v_shift, 16)
                sp_.dma_start(v1s[64:128, 1:TT, :], v1[0:64, 1:TT, :]).then_inc(v_shift, 16)
            w_o = (io["even_w_out"], io["odd_w_o"])[layer][0]
            for j in range(2 * layer, N_OUT):
                load_cols(U_OUT[layer] + j, w_o, 256 * j)
            if layer == 1:
                sp_.dma_start(last_gain[:], io["norm_ffn_post"][1:2, :].broadcast_to([P, D])).then_inc(last_gain_in, 16)
            w_up = io["ffn_w_up"][layer]

            def load_up(u, j, i=None):
                slot_free(u, i, RING)
                for b in range(2):
                    load(u, cols(w_up, j * P + F * b, P), w_raw[u % RING][:, :, b, :])

            for j in range(2):
                load_up(U_UP[layer] + j, j)
            with sp_.Fori(0, 6) as i:
                for j in range(RING):
                    load_up(U_UP[layer] + 2 + j, i * RING + (2 + j), i)
            for j in range(20, FT):
                load_up(U_UP[layer] + j, j)
            w_down = io["ffn_w_down"][layer]
            with sp_.Fori(0, 4) as i:
                for c, (k0, k1) in enumerate(DOWN_K):
                    u = U_DOWN[layer] + c
                    slot_free(u, i, RING)
                    src = w_down[k0 * P:k1 * P, bass.ds(i * 256, 256)].rearrange("(k p) n -> p k n", p=P)
                    load(u, src, whole(u % RING, k1 - k0))
        for t in range(TT):
            for h in range(2):
                half = slice(h * D // 2, (h + 1) * D // 2)
                sp_.wait_ge(out_done, 2 * t + h + 1)
                sp_.dma_start(out[0, P * t:P * t + P, half], m_tok[:, t, half]).then_inc(stored, 16)
        sp_.wait_ge(stored, 16 * 2 * TT)

    @block.gpsimd
    def _(pool):
        pool.memset(gate_w[:], 0.0).then_inc(zeroed, 1)
        for n in range(7):
            if n == 5:
                pool.wait_ge(rope_raw, 2)
                for a in range(2):
                    pool.memset(kz[a][HD * (1 - a):HD * (1 - a) + HD], 0.0).then_inc(kz_zeroed, 1)
            for i in range(1, N_SUMS + 1):
                pool.wait_ge(sq_done, DT * n + i + 1)
                if i == 1:
                    if n:
                        pool.wait_ge(ms_mm, n)
                    ins = pool.tensor_tensor(sumsq[:], sq[0][:], sq[1][:], ALU.add)
                else:
                    pool.wait_ge(sum_done, N_SUMS * n + i - 1)
                    ins = pool.tensor_tensor(sumsq[:], sumsq[:], sq[i % 2][:], ALU.add)
                ins.then_inc(sum_done, 1)

    @block.scalar
    def _(act):
        def split_hi(u, k=UK, i=None, per=RING, cnt=0):
            s = u % RING
            at_ = loaded_at(u)
            act.wait_ge(w_loaded[s], at_ if i is None else i * cnt + at_)
            act.activation(w_hi[s][:, 0:k], w_raw[s][:, 0:k], ACT.Copy).then_inc(w_hi_done, 1)

        def square(n, i, src):
            if i >= 2:
                act.wait_ge(sum_done, N_SUMS * n + max(1, i - 2))
            elif n:
                act.wait_ge(ms_mm, n)
            act.activation(sq[i % 2][:], src, ACT.Square).then_inc(sq_done, 1)

        def root(n):
            act.wait_ge(ms_mm, n + 1)
            act.activation(std[:], bank(7)[:, 0:TT], ACT.Sqrt, scale=1.0 / D, bias=eps).then_inc(std_done, 1)

        eps = narrow[:, 9, 0:1]

        def first_split_hi(n):
            u, ks = first_piece(n)
            act.wait_ge(first_in[n], 16)
            act.activation(w_hi[u][:, ks], w_raw[u][:, ks], ACT.Copy).then_inc(piece_signal(n, first_hi, w_hi_done), 1)

        for i in range(DT):
            if i == 0:
                act.wait_ge(vec_done, 1)
            act.wait_ge(xt_copied, i + 1)
            act.activation(hx_hi[:, i, :], x[:, i, :], ACT.Identity, scale=gain(0, 0, i)).then_inc(hx_hi_done, 1)
            if i % 2 == 0:
                first_split_hi(i)
                first_split_hi(i + 1)
            square(0, i, x[:, i, :])
        split_hi(2)
        root(0)
        act.wait_ge(setup_v, 1)
        act.activation(narrow[:, 1, 0:LT], narrow[:, 0, 0:LT], ACT.Exp, scale=-1.0).then_inc(setup_a, 1)

        def sines():
            act.wait_ge(setup_v, 3)
            act.activation(sin_t[:], ang[:], ACT.Sin).then_inc(setup_a, 1)
            act.activation(cos_t[:], angc[:], ACT.Sin).then_inc(setup_a, 1)


        def sb_softplus(h):
            b = h % 2
            act.wait_ge(z_copied, h + 1)
            if h >= 2:
                act.wait_ge(cum_mm, h - 1)
            act.activation(sp[b][:], z_s[h % 4][:], ACT.Abs).then_inc(abs_done, 1)
            act.wait_ge(abs_done, h + 1)
            act.activation(sp[b][:], sp[b][:], ACT.Exp, scale=-1.0).then_inc(exp_done, 1)
            act.wait_ge(exp_done, h + 1)
            act.activation(sp[b][:], sp[b][:], ACT.Ln, bias=1.0).then_inc(ln_done, 1)

        def sb_weights(h):
            act.wait_ge(t_done, h + 1)
            act.activation(z_s[h % 4][:], z_s[h % 4][:], ACT.Exp).then_inc(w_done, 1)

        def sb_out(ti):
            act.wait_ge(av_mm, 2 * ti + 2)
            act.activation(y_hi[:, LT + ti, :], bank(6 + ti % 2), ACT.Copy).then_inc(y_hi_done, 1)

        def sb_hi(h):
            act.wait_ge(sp_done, h + 1)
            act.activation(sp_hi[h % 2][:], sp[h % 2][:], ACT.Copy).then_inc(sp_hi_done, 1)

        act.wait_ge(vec_done, 2)
        for u in range(N_IN):
            g = group_of(u)
            if u < 2:
                act.wait_ge(group_evac, g + 1)
                for b in range(2):
                    t = 2 * u + b
                    act.activation(xc[:, t, :], (ug, uv)[b][:], ACT.Identity, scale=col(V_CONV + 12 + t),
                                   bias=col(V_CONVB + t)).then_inc(xc_center, 1)
            if u != 2:
                split_hi(u + (3 if u < 2 else 2))
            if 2 <= u < 6:
                t = u - 2
                for b, (dst, bias) in enumerate(((lru_r, V_BA), (lru_i, V_BX))):
                    act.wait_ge(gate_mm, 2 * t + b + 1)
                    act.activation(dst[:, t, :], bank(6 + b), ACT.Sigmoid, bias=col(bias + t)).then_inc(gate_act, 1)
            if u == 4:
                sines()
            if u == 5:
                act.wait_ge(setup_v, 2)
                act.wait_ge(gate_act, 2 * LT)
                for t in range(LT):
                    act.activation(lru_a[:, t, :], lru_r[:, t, :], ACT.Exp, scale=nlam[:, t:t + 1]).then_inc(lru_act, 1)
                for t in range(LT):
                    act.activation(lru_th[:, t, :], lru_r[:, t, :], ACT.Tanh, scale=plam[:, t:t + 1]).then_inc(lru_act, 1)
            if u == 6:
                act.wait_ge(lru_dve, 3)
                act.activation(lru_r[:], lru_r[:], ACT.Sqrt).then_inc(lru_act, 1)
                act.activation(gr[:], gr[:], ACT.Gelu_apprx_tanh).then_inc(lru_act, 1)
                act.preload_act_table_set("natural_log_exp_and_others")
            if u == 7:
                act.wait_ge(lru_dve, 4 + LT + 1)
                act.activation(y_hi[:, 0:LT, :], lru_r[:], ACT.Copy).then_inc(y_hi_done, 1)
            if u == 8:
                sb_softplus(0)
                sb_hi(0)
        sb_softplus(1)

        for h in range(SB_HEADS):
            if h + 1 < SB_HEADS:
                sb_hi(h + 1)
            sb_weights(h)
            if h + 2 < SB_HEADS:
                sb_softplus(h + 2)
            if h >= 3 and h % 2 == 1:
                sb_out((h - 3) // 2)
            if h == 2:
                split_hi(U_OUT[0] + 2)
        sb_out(SB_HEADS // 2 - 1)

        def boundary(bi, n, which, layer, u):
            root(n)
            for i in range(DT):
                act.wait_ge(x_new, DT * bi + i + 1)
                act.activation(hx_hi[:, i, :], x[:, i, :], ACT.Identity, scale=gain(which, layer, i)).then_inc(hx_hi_done, 1)
                square(n + 1, i, x[:, i, :])
            split_hi(u + 2)
            root(n + 1)

        def out_projection(layer, n):
            for j in range(N_OUT):
                u = U_OUT[layer] + j
                split = j > 0
                if j == N_OUT - 1:
                    act.preload_act_table_set("sqrt_and_others")
                    split_hi(u + 2)
                for b in range(2):
                    m_squares(n, u, j, b)
                if split and j < N_OUT - 1:
                    split_hi(u + 2)

        def m_squares(n, u, mp, b):
            if b == 0:
                act.wait_ge(m_first, 4 * (n // 2) + mp + 1)
            else:
                act.wait_ge(unit_done, u + 1)
            square(n, 2 * mp + b, bank(group_banks(group_of(u)) + b))

        def ffn_up(layer, j, u, i=None):
            f = FT * layer + j
            g = group_of(u)
            act.wait_ge(scaled, f + 1)
            if i is not None or j or layer:
                act.wait_ge(prod_done, f)
            act.activation(cg[:], ug[:], ACT.Identity, scale=col(ffn_vec(layer, 2, j)), bias=col(ffn_vec(layer, 3, j))).then_inc(center, 1)
            act.wait_ge(group_evac, evacuated(g) if i is None else i * RING + evacuated(g))
            if i is not None or j or layer:
                act.wait_ge(g_ready, f)
            act.activation(cv[:], uv[:], ACT.Identity, scale=col(ffn_vec(layer, 2, j + FT)), bias=col(ffn_vec(layer, 3, j + FT))).then_inc(center, 1)
            v = split_at(layer, u)
            if v is not None:
                split_hi(v, i=i, cnt=32)
            act.wait_ge(tapped, 4 * f + 3)
            act.activation(cg[:], cg[:], ACT.Gelu_apprx_tanh).then_inc(gelu_done, 1)
            act.wait_ge(prod_done, f + 1)
            act.activation(tile_(g_hi, j), cv[:], ACT.Copy).then_inc(g_hi_done, 1)

        def token_squares(u, mp, b):
            if b == 0:
                act.wait_ge(mtok_mm, mp + 1)
                if mp:
                    act.wait_ge(mtok_sq, TT * mp)
            else:
                act.wait_ge(unit_done, u + 1)
            for t in (2 * b, 2 * b + 1):
                c0 = T * group_banks(group_of(u)) + 256 * t
                act.activation(sq[b][:, 256 * (t % 2):256 * (t % 2) + 256], ps[:, c0:c0 + 256], ACT.Square, accum_out=narrow[:, t, mp:mp + 1]).then_inc(mtok_sq, 1)

        def ffn(layer):
            for j in range(3):
                ffn_up(layer, j, U_UP[layer] + j)
            with act.Fori(0, 5) as i:
                for j in range(RING):
                    ffn_up(layer, i * RING + (3 + j), U_UP[layer] + 3 + j, i)
            for j in range(18, FT):
                ffn_up(layer, j, U_UP[layer] + j)
            for mp in range(4):
                for c in range(3):
                    u = U_DOWN[layer] + 3 * mp + c
                    v = u + 2
                    if v < U_DOWN[layer] + N_DOWN:
                        k0, k1 = DOWN_K[(3 * mp + c + 2) % 3]
                        split_hi(v, k1 - k0)
                    elif v < N_UNITS:
                        split_hi(v)
                    if c == 2 and mp == 3:
                        act.preload_act_table_set("sqrt_and_others")
                    if c == 2:
                        for b in range(2):
                            if layer == 0:
                                m_squares(3, u, mp, b)
                            else:
                                token_squares(u, mp, b)
                    if layer == 1 and mp < 2 and c < 2:
                        for i in range(4 * mp + 2 * c, 4 * mp + 2 * c + 2):
                            act.wait_ge(xtok_mm, i + 1)
                            act.activation(x_tok[:, :, P * i:P * i + P], bank(6 + i % 2).rearrange("p (t c) -> p t c", c=P),
                                           ACT.Copy).then_inc(xtok_copied, 1)

        out_projection(0, 1)
        boundary(0, 1, 2, 0, U_UP[0])
        ffn(0)
        boundary(1, 3, 0, 1, U_QKV)
        swap_halves(act, 0, 1)
        split_hi(U_QKV + 3)
        swap_halves(act, 1, 1)
        for k in range(2, N_QKV - 1):
            split_hi(U_QKV + k + 2)
            swap_halves(act, k, 1)

        for c in range(NCH + 2):
            if c < NCH:
                kw = HD if c == 0 else P
                o = 4 * (c % 2)
                act.wait_ge(negm_done, c + 1)
                if c >= 2:
                    act.wait_ge(pt_mm, 2 * (c - 1))
                bk = bank(sw_banks(c), 2).rearrange("p (e k) -> p e k", k=P)
                for e in range(8):
                    act.activation(prob[c % 2][:, e, 0:kw], bk[:, e, 0:kw], ACT.Exp, bias=narrow[:, o, e:e + 1],
                                   accum_out=narrow[:, o + 1, e:e + 1]).then_inc(p_done, 1)
                act.activation(narrow[:, o + 2, 0:8], narrow[:, o + 3, 0:8], ACT.Exp).then_inc(ex_done, 1)
            if c == 0:
                act.wait_ge(unit_done, U_QKV + N_QKV)
                for t in range(TT):
                    c0 = T * group_banks(group_of(U_QKV + N_QKV - 1)) + 256 * t
                    act.activation(v1[:, t, :], ps[:, c0:c0 + 256], ACT.Identity, scale=rcol[:, t:t + 1]).then_inc(v_raw, 1)
            if c < 2:
                split_hi(U_OUT[1] + 1 + c)
            if 1 <= c <= NCH:
                d = c - 1
                kw = HD if d == 0 else P
                for q in range(2):
                    act.wait_ge(pt_mm, 2 * d + q + 1)
                    if d >= 2:
                        act.wait_ge(o_mm, d - 1)
                    act.activation(probT[d % 2][0:kw, 4 * q:4 * q + 4, :], bank(4 + q).rearrange("p (e k) -> p e k", k=P)[0:kw],
                                   ACT.Copy).then_inc(pt_copied, 1)
            if c >= 2:
                d = c - 2
                act.wait_ge(o_mm, d + 1)
                act.activation(y_hi[:, :, CHUNK * d:CHUNK * d + CHUNK],
                               bank(6 + d % 2).rearrange("p (k t) -> p k t", t=CHUNK), ACT.Copy).then_inc(y_hi_done, 1)
        out_projection(1, 5)
        boundary(2, 5, 2, 1, U_UP[1])
        ffn(1)
        for b in range(2):
            act.wait_ge(tok_sum, b + 1)
            act.activation(std[:, 2 * b:2 * b + 2], narrow[:, 2 * b:2 * b + 2, 4], ACT.Sqrt, scale=1.0 / D, bias=eps).then_inc(tok_std, 1)

    @block.vector
    def _(dve):
        def split_lo(u, k=UK, i=None):
            s = u % RING
            dve.wait_ge(w_hi_done, u + 1 if i is None else i * RING + (u + 1))
            dve.tensor_tensor(w_lo[s][:, 0:k], w_raw[s][:, 0:k], w_hi[s][:, 0:k], ALU.subtract).then_inc(w_lo_done, 1)

        def inverse_rms(n):
            dve.wait_ge(std_done, n + 1)
            if n:
                dve.wait_ge(diag_done, n)
            dve.reciprocal(rcol[:], std[:]).then_inc(rcol_done, 1)
            dve.wait_ge(rcol_done, n + 1)
            for t in range(TT):
                ins = dve.tensor_scalar(diag[:, t, :], ident, rcol[:, t:t + 1], None, ALU.mult)
            ins.then_inc(diag_done, 1)

        def spread(n):
            dve.wait_ge(bc_mm, n + 1)
            dve.tensor_copy(rbc[:], bank(6)).then_inc(rbc_done, 1)

        dve.memset(narrow[:, 9, 0:1], EPS)
        dve.wait_ge(const_in, 16)
        dve.tensor_copy(tri_r[:], tri)
        dve.tensor_copy(ones_r[:], ones)
        dve.tensor_copy(ident_b[:], ident)
        dve.tensor_copy(mask_b[:], mask).then_inc(consts_cast, 1)

        def first_split_lo(n):
            u, ks = first_piece(n)
            piece_wait(dve, n, first_hi, w_hi_done)
            dve.tensor_tensor(w_lo[u][:, ks], w_raw[u][:, ks], w_hi[u][:, ks], ALU.subtract).then_inc(piece_signal(n, first_lo, w_lo_done), 1)

        dve.wait_ge(vec_mm, 1)
        dve.tensor_copy(vec[:, 0:16], bank(5)[:, 0:16]).then_inc(vec_done, 1)
        dve.wait_ge(vec_done, 1)
        for i in range(DT):
            dve.wait_ge(xt_mm, i + 1)
            dve.tensor_copy(x[:, i, :], bank(6 + i % 2)).then_inc(xt_copied, 1)
            dve.wait_ge(hx_hi_done, i + 1)
            dve.scalar_tensor_tensor(out=hx_lo[:, i, :], in0=x[:, i, :], scalar=gain(0, 0, i), in1=hx_hi[:, i, :],
                                     op0=ALU.mult, op1=ALU.subtract).then_inc(hx_ready, 1)
            if i % 2 == 0:
                first_split_lo(i)
                first_split_lo(i + 1)
        dve.wait_ge(vec_mm, 2)
        dve.tensor_copy(vec[:, 16:V_ROWS0 + 2 * V_ROWSF], bank(5)[:, 16:V_ROWS0 + 2 * V_ROWSF]).then_inc(vec_done, 1)
        dve.wait_ge(vec_done, 2)
        lam = vec[:, V_LAM:V_LAM + LT]
        dve.scalar_tensor_tensor(out=narrow[:, 0, 0:LT], in0=lam, scalar=-1.0, in1=lam, op0=ALU.mult, op1=ALU.max).then_inc(setup_v, 1)
        split_lo(2)
        inverse_rms(0)
        spread(0)

        chain = sem("setup_chain")
        made = [0]

        def step(ins):
            made[0] += 1
            ins.then_inc(chain, 1)
            dve.wait_ge(chain, made[0])

        def rotary_angles():
            c1 = 6.28125
            c2 = float(np.float32(np.int64((2 * np.pi - c1) * 2 ** 20) / 2.0 ** 20))
            c3 = float(2 * np.pi - c1 - c2)
            magic = 12582912.0
            pi = float(np.nextafter(np.float32(np.pi), np.float32(0)))
            dve.wait_ge(pos_in, 16)
            step(dve.tensor_copy(ang[:], pos_i[:]))
            step(dve.tensor_scalar(ang[:], ang[:], inv_freq, None, ALU.mult))
            step(dve.tensor_scalar(turns[:], ang[:], float(1 / (2 * np.pi)), magic, ALU.mult, ALU.add))
            step(dve.tensor_scalar(turns[:], turns[:], -magic, None, ALU.add))
            for c in (c1, c2, c3):
                step(dve.scalar_tensor_tensor(out=ang[:], in0=turns[:], scalar=-c, in1=ang[:], op0=ALU.mult, op1=ALU.add))
            step(dve.tensor_scalar(turns[:], ang[:], float(np.pi / 2), -2 * float(np.pi), ALU.is_gt, ALU.mult))
            step(dve.scalar_tensor_tensor(out=angc[:], in0=ang[:], scalar=float(np.pi / 2), in1=turns[:], op0=ALU.add, op1=ALU.add))
            step(dve.tensor_scalar(ang[:], ang[:], pi, -pi, ALU.min, ALU.max))
            dve.tensor_scalar(angc[:], angc[:], pi, -pi, ALU.min, ALU.max).then_inc(setup_v, 1)

        def softplus_lambda():
            e, s, s2, q = (narrow[:, r, 0:LT] for r in (1, 2, 3, 4))
            dve.wait_ge(setup_a, 1)
            step(dve.tensor_scalar(s, e, 2.0, None, ALU.add))
            step(dve.reciprocal(s, s))
            step(dve.tensor_tensor(s, s, e, ALU.mult))
            step(dve.tensor_tensor(s2, s, s, ALU.mult))
            step(dve.tensor_scalar(q, s2, 1.0 / 17, None, ALU.mult))
            for k in (15, 13, 11, 9, 7, 5, 3):
                step(dve.scalar_tensor_tensor(out=q, in0=q, scalar=1.0 / k, in1=s2, op0=ALU.add, op1=ALU.mult))
            step(dve.scalar_tensor_tensor(out=q, in0=q, scalar=1.0, in1=s, op0=ALU.add, op1=ALU.mult))
            step(dve.tensor_scalar(s, vec[:, V_LAM:V_LAM + LT], -1.0, 0.0, ALU.mult, ALU.max))
            step(dve.scalar_tensor_tensor(out=q, in0=q, scalar=2.0, in1=s, op0=ALU.mult, op1=ALU.add))
            step(dve.tensor_scalar(plam[:], q, 8.0, None, ALU.mult))
            dve.tensor_scalar(nlam[:], q, -8.0, None, ALU.mult).then_inc(setup_v, 1)

        def rotary_signs():
            dve.wait_ge(setup_a, 3)
            step(dve.tensor_scalar(sin_t[:], sin_t[:], rope_sign, None, ALU.mult))
            dve.wait_ge(sink_in, 16)
            v = sink_row[:].rearrange("p (k g h) -> p g k h", g=2, h=2)
            for g in range(2):
                step(dve.tensor_copy(sink[64 * g:64 * g + 64, :].rearrange("p (h k) -> p k h", h=2), v[64 * g:64 * g + 64, g]))

        def lru_inputs():
            dve.wait_ge(gate_act, 2 * LT)
            dve.tensor_tensor(lru_i[:], lru_i[:], xc[:], ALU.mult).then_inc(lru_dve, 1)
            dve.wait_ge(lru_act, 2 * LT)
            dve.tensor_tensor(lru_r[:], lru_a[:], lru_a[:], ALU.mult).then_inc(lru_dve, 1)
            dve.wait_ge(lru_dve, 2)
            dve.scalar_tensor_tensor(out=lru_r[:], in0=lru_r[:], scalar=1.0, in1=lru_th[:], op0=ALU.add, op1=ALU.mult).then_inc(lru_dve, 1)

        def lru_scan():
            dve.wait_ge(lru_act, 2 * LT + 1)
            dve.tensor_tensor(lru_i[:], lru_i[:], lru_r[:], ALU.mult).then_inc(lru_dve, 1)
            dve.wait_ge(lru_dve, 4)
            for t in range(LT):
                dve.tensor_tensor_scan(out=xc[:, t, :], data0=lru_a[:, t, :], data1=lru_i[:, t, :], initial=0.0,
                                       op0=ALU.mult, op1=ALU.add).then_inc(lru_dve, 1)
            dve.wait_ge(lru_act, 2 * LT + 2)
            dve.wait_ge(lru_dve, 4 + LT)
            dve.tensor_tensor(lru_r[:], xc[:], gr[:], ALU.mult).then_inc(lru_dve, 1)

        def sb_z(h):
            dve.wait_ge(z_mm, h + 1)
            if h >= 4:
                dve.wait_ge(av_mm, h - 3)
            dve.tensor_copy(z_s[h % 4][:], bank(0, 3)[:, 0:SPAN]).then_inc(z_copied, 1)

        def sb_t(h):
            dve.wait_ge(cum_mm, h + 1)
            dve.tensor_tensor(z_s[h % 4][:], z_s[h % 4][:], bank(3, 3)[:, 0:SPAN], ALU.subtract).then_inc(t_done, 1)

        def sb_out(ti):
            dve.wait_ge(y_hi_done, 1 + ti + 1)
            dve.tensor_tensor(y_lo[:, LT + ti, :], bank(6 + ti % 2), y_hi[:, LT + ti, :], ALU.subtract).then_inc(y_ready, 1)

        def sb_softplus(h):
            dve.wait_ge(ln_done, h + 1)
            dve.scalar_tensor_tensor(out=sp[h % 2][:], in0=z_s[h % 4][:], scalar=0.0, in1=sp[h % 2][:], op0=ALU.max, op1=ALU.add).then_inc(sp_done, 1)

        def sb_lo(h):
            dve.wait_ge(sp_hi_done, h + 1)
            dve.tensor_tensor(sp_lo[h % 2][:], sp[h % 2][:], sp_hi[h % 2][:], ALU.subtract).then_inc(sp_lo_done, 1)

        for u in range(N_IN):
            g = group_of(u)
            dve.wait_ge(unit_done, u + 1)
            if u == 0:
                dve.wait_ge(rbc_done, 1)
            b0 = group_banks(g)
            if u < 2:
                if u:
                    dve.wait_ge(xc_tap, 6 * u)
                for b in range(2):
                    ins = dve.tensor_tensor((ug, uv)[b][:], bank(b0 + b), rbc[:], ALU.mult)
                ins.then_inc(group_evac, 1)
                for s in range(1, 4):
                    for b in range(2):
                        t = 2 * u + b
                        if s == 1:
                            dve.wait_ge(xc_center, 2 * u + b + 1)
                        else:
                            dve.wait_ge(xc_tap, 6 * u + 2 * (s - 2) + b + 1)
                        dve.scalar_tensor_tensor(out=xc[:, t, s:], in0=(ug, uv)[b][:, 0:T - s], scalar=col(V_CONV + 4 * (3 - s) + t),
                                                 in1=xc[:, t, s:], op0=ALU.mult, op1=ALU.add).then_inc(xc_tap, 1)
            elif u < 8:
                dst = {1: gr, 2: qT, 3: kT}[u // 2]
                for b in range(2):
                    t = 2 * (u % 2) + b
                    if u // 2 == 2:
                        ins = dve.scalar_tensor_tensor(out=dst[:, t, :], in0=bank(b0 + b), scalar=SCALE, in1=rbc[:], op0=ALU.mult, op1=ALU.mult)
                    else:
                        ins = dve.tensor_tensor(dst[:, t, :], bank(b0 + b), rbc[:], ALU.mult)
                ins.then_inc(group_evac, 1)
            else:
                for t in range(TT):
                    c = T * b0 + 256 * t
                    ins = dve.tensor_scalar(v0[:, t, 256 * (u - 8):256 * (u - 8) + 256], ps[:, c:c + 256], rcol[:, t:t + 1], None, ALU.mult)
                ins.then_inc(group_evac, 1)
            if u != 2:
                split_lo(u + (3 if u < 2 else 2))
            if u == 2:
                softplus_lambda()
            if u == 3:
                rotary_angles()
            if u == 5:
                rotary_signs()
                lru_inputs()
            if u == 6:
                lru_scan()
            if u == 7:
                dve.wait_ge(y_hi_done, 1)
                dve.tensor_tensor(y_lo[:, 0:LT, :], lru_r[:], y_hi[:, 0:LT, :], ALU.subtract).then_inc(y_ready, 1)
            if u == 8:
                dve.wait_ge(y_ready, 1)
                sb_z(0)
                sb_softplus(0)
                sb_lo(0)
                sb_z(1)
        for h in range(SB_HEADS):
            if h + 1 < SB_HEADS:
                sb_softplus(h + 1)
            sb_t(h)
            if h + 2 < SB_HEADS:
                sb_z(h + 2)
            if h + 1 < SB_HEADS:
                sb_lo(h + 1)
            if h >= 3 and h % 2 == 1:
                sb_out((h - 3) // 2)
            if h == 2:
                split_lo(U_OUT[0] + 2)
        sb_out(SB_HEADS // 2 - 1)

        def m_copy(n, u, mp, pair):
            for b in range(2):
                dve.wait_ge(sq_done, DT * n + 2 * mp + b + 1)
                ins = dve.tensor_copy(m[:, 2 * mp + b, :], bank(pair + b))
            ins.then_inc(group_evac, 1)

        def out_projection(layer, n):
            for j in range(N_OUT):
                u = U_OUT[layer] + j
                if j == N_OUT - 1:
                    split_lo(u + 2)
                m_copy(n, u, j, group_banks(group_of(u)))
                if 0 < j < N_OUT - 1:
                    split_lo(u + 2)

        def boundary(bi, n, post, pre, u):
            inverse_rms(n)
            dve.wait_ge(bc_mm, n + 1)

            def normed(i):
                dve.scalar_tensor_tensor(out=m[:, i, :], in0=m[:, i, :], scalar=gain(*post, i), in1=bank(6),
                                         op0=ALU.mult, op1=ALU.mult).then_inc(post_t, 1)

            def add(i):
                dve.wait_ge(post_t, DT * bi + i + 1)
                dve.tensor_tensor(x[:, i, :], x[:, i, :], m[:, i, :], ALU.add).then_inc(x_new, 1)

            def lo(i):
                dve.wait_ge(hx_hi_done, DT * (bi + 1) + i + 1)
                dve.scalar_tensor_tensor(out=hx_lo[:, i, :], in0=x[:, i, :], scalar=gain(*pre, i), in1=hx_hi[:, i, :],
                                         op0=ALU.mult, op1=ALU.subtract).then_inc(hx_ready, 1)

            normed(0)
            add(0)
            for i in range(DT):
                if i + 1 < DT:
                    normed(i + 1)
                lo(i)
                if i + 1 < DT:
                    add(i + 1)
            split_lo(u + 2)
            inverse_rms(n + 1)
            spread(n + 1)
            dve.wait_ge(rbc_done, (n + 1) // 2 + 1)

        def ffn_up(layer, j, u, i=None):
            f = FT * layer + j
            g = group_of(u)
            b0 = group_banks(g)
            dve.wait_ge(unit_done, u + 1 if i is None else i * RING + (u + 1))
            if i is not None or j or layer:
                dve.wait_ge(tapped, 4 * f)
            dve.tensor_tensor(ug[:], bank(b0), rbc[:], ALU.mult).then_inc(scaled, 1)
            dve.tensor_tensor(uv[:], bank(b0 + 1), rbc[:], ALU.mult).then_inc(group_evac, 1)
            for s in (1, 2):
                for b, (src, dst) in enumerate(((ug, cg), (uv, cv))):
                    if s == 1:
                        dve.wait_ge(center, 2 * f + b + 1)
                    else:
                        dve.wait_ge(tapped, 4 * f + b + 1)
                    dve.scalar_tensor_tensor(out=dst[:, s:], in0=src[:, 0:T - s], scalar=col(ffn_vec(layer, 2 - s, j + FT * b)),
                                             in1=dst[:, s:], op0=ALU.mult, op1=ALU.add).then_inc(tapped, 1)
            v = split_at(layer, u)
            if v is not None:
                split_lo(v, i=i)
            dve.wait_ge(gelu_done, f + 1)
            dve.wait_ge(tapped, 4 * f + 4)
            dve.tensor_tensor(cv[:], cg[:], cv[:], ALU.mult).then_inc(prod_done, 1)
            dve.wait_ge(g_hi_done, f + 1)
            dve.tensor_tensor(tile_(g_lo, j), cv[:], tile_(g_hi, j), ALU.subtract).then_inc(g_ready, 1)

        def token_gains(u, mp, b):
            if mp == b == 0:
                dve.wait_ge(last_gain_in, 16)
            dve.wait_ge(mtok_sq, TT * mp + 2 * b + 2)
            ts = slice(2 * b, 2 * b + 2)
            if mp == 3:
                dve.tensor_reduce(narrow[:, ts, 4], narrow[:, ts, 0:4], AX.X, ALU.add).then_inc(tok_sum, 1)
            g = last_gain[:, 256 * mp:256 * mp + 256].unsqueeze(1).broadcast_to([P, 2, 256])
            dve.tensor_tensor(m_tok[:, ts, 256 * mp:256 * mp + 256], bank(group_banks(group_of(u)) + b).rearrange("p (t c) -> p t c", t=2),
                              g, ALU.mult).then_inc(mtok_done, 1)
            if mp < 3:
                return
            dve.wait_ge(tok_std, b + 1)
            dve.reciprocal(rcol[:, ts], std[:, ts]).then_inc(tok_rms, 1)
            dve.wait_ge(tok_rms, b + 1)
            dve.wait_ge(mtok_done, 2 * mp + b + 1)
            dve.wait_ge(xtok_copied, DT)
            for t in (2 * b, 2 * b + 1):
                for h in range(2):
                    half = slice(h * D // 2, (h + 1) * D // 2)
                    dve.scalar_tensor_tensor(out=m_tok[:, t, half], in0=m_tok[:, t, half], scalar=rcol[:, t:t + 1],
                                             in1=x_tok[:, t, half], op0=ALU.mult, op1=ALU.add).then_inc(out_done, 1)

        def ffn(layer):
            for j in range(3):
                ffn_up(layer, j, U_UP[layer] + j)
            with dve.Fori(0, 5) as i:
                for j in range(RING):
                    ffn_up(layer, i * RING + (3 + j), U_UP[layer] + 3 + j, i)
            for j in range(18, FT):
                ffn_up(layer, j, U_UP[layer] + j)
            for mp in range(4):
                for c in range(3):
                    u = U_DOWN[layer] + 3 * mp + c
                    v = u + 2
                    if v < U_DOWN[layer] + N_DOWN:
                        k0, k1 = DOWN_K[(3 * mp + c + 2) % 3]
                        split_lo(v, k1 - k0)
                    elif v < N_UNITS:
                        split_lo(v)
                    if c == 2 and layer == 0:
                        m_copy(3, u, mp, group_banks(group_of(u)))
                    if c == 2 and layer == 1:
                        for b in range(2):
                            token_gains(u, mp, b)

        out_projection(0, 1)
        boundary(0, 1, (1, 0), (2, 0), U_UP[0])
        ffn(0)
        boundary(1, 3, (3, 0), (0, 1), U_QKV)

        def raw(i):
            u = U_QKV + i
            b0 = group_banks(group_of(u))
            dve.wait_ge(unit_done, u + 1)
            if i >= 2:
                dve.wait_ge(rope_done, 2 * i)
            for b in range(2):
                if i == 0:
                    ins = dve.tensor_tensor(rp[0][b][:], bank(b0 + b), rbc[:], ALU.mult)
                else:
                    ins = dve.scalar_tensor_tensor(out=rp[i % 2][b][:], in0=bank(b0 + b), scalar=SCALE, in1=rbc[:], op0=ALU.mult, op1=ALU.mult)
                ins.then_inc(rope_raw, 1)

        def rope_finish(i):
            r, sw = rp[i % 2], rsw[i % 2]
            for b in range(2):
                dve.wait_ge(rope_sw[i % 2][b], 64 * (i // 2 + 1))
                dve.tensor_tensor(r[b][:], r[b][:], cos_t[:], ALU.mult).then_inc(rope_mul, 1)
                dve.tensor_tensor(sw[b][:], sw[b][:], sin_t[:], ALU.mult).then_inc(rope_mul, 1)
            for b in range(2):
                dve.wait_ge(rope_mul, 4 * i + 2 * b + 2)
                if i == 0:
                    for h in range(2):
                        hh = slice(HD * h, HD * h + HD)
                        dve.tensor_tensor(kz[h][hh, 2 * b + h, :], r[b][hh, :], sw[b][hh, :], ALU.add).then_inc(rope_done, 1)
                else:
                    chunks = [t[b][:].rearrange("p (c t) -> p c t", t=CHUNK) for t in (r, sw)]
                    dve.tensor_tensor(qr[:, i - 1, :, b, :], chunks[0], chunks[1], ALU.add).then_inc(rope_done, 1)

        raw(0)
        raw(1)
        split_lo(U_QKV + 3)
        rope_finish(0)
        raw(2)
        split_lo(U_QKV + 4)
        rope_finish(1)
        split_lo(U_QKV + 5)
        raw(3)
        rope_finish(2)
        raw(4)
        rope_finish(3)
        rope_finish(4)

        def max_steps(c):
            return 4 * c

        def norm_steps(c):
            return 4 * c + 2

        def sw_max(c):
            kw = HD if c == 0 else P
            o = 4 * (c % 2)
            dve.wait_ge(s_mm, c + 1)
            bk = bank(sw_banks(c), 2).rearrange("p (e k) -> p e k", k=P)
            if c >= 2:
                dve.wait_ge(ex_done, c - 1)
            dve.tensor_reduce(narrow[:, o, 0:8], bk[:, :, 0:kw], AX.X, ALU.max).then_inc(smax_done, 1)
            dve.wait_ge(smax_done, c + 1)
            dve.tensor_tensor(narrow[:, o, 0:8], narrow[:, o, 0:8], sink[:], ALU.max).then_inc(sw_step, 1)
            dve.wait_ge(sw_step, max_steps(c) + 1)
            dve.tensor_tensor(narrow[:, o + 3, 0:8], sink[:], narrow[:, o, 0:8], ALU.subtract).then_inc(sw_step, 1)
            dve.tensor_scalar(narrow[:, o, 0:8], narrow[:, o, 0:8], -1.0, None, ALU.mult).then_inc(negm_done, 1)

        def sw_norm(c):
            kw = HD if c == 0 else P
            o = 4 * (c % 2)
            dve.wait_ge(ex_done, c + 1)
            dve.tensor_tensor(narrow[:, o + 1, 0:8], narrow[:, o + 1, 0:8], narrow[:, o + 2, 0:8], ALU.add).then_inc(sw_step, 1)
            dve.wait_ge(sw_step, norm_steps(c) + 1)
            dve.reciprocal(narrow[:, o + 1, 0:8], narrow[:, o + 1, 0:8]).then_inc(sw_step, 1)
            dve.wait_ge(sw_step, norm_steps(c) + 2)
            pr = prob[c % 2][:, :, 0:kw]
            dve.tensor_tensor(pr, pr, narrow[:, o + 1, 0:8].unsqueeze(2).broadcast_to([P, 8, kw]), ALU.mult).then_inc(pn_done, 1)

        def sw_lo(c):
            dve.wait_ge(y_hi_done, 1 + LT + c + 1)
            ys = slice(CHUNK * c, CHUNK * c + CHUNK)
            dve.tensor_tensor(y_lo[:, :, ys], bank(6 + c % 2).rearrange("p (k t) -> p k t", t=CHUNK), y_hi[:, :, ys], ALU.subtract).then_inc(y_ready, 1)

        sw_max(0)
        split_lo(U_OUT[1])
        for c in range(NCH):
            sw_norm(c)
            if c + 1 < NCH:
                sw_max(c + 1)
            if c >= 2:
                sw_lo(c - 2)
            if c < 2:
                split_lo(U_OUT[1] + 1 + c)
        sw_lo(NCH - 2)
        sw_lo(NCH - 1)

        out_projection(1, 5)
        boundary(2, 5, (1, 1), (2, 1), U_UP[1])
        ffn(1)

    @block.tensor
    def _(pe):
        def three(dst, s_hi, s_lo, r_hi, r_lo, first, last):
            pe.matmul(dst, s_hi, r_hi, start=first, stop=False)
            pe.matmul(dst, s_hi, r_lo, start=False, stop=False)
            return pe.matmul(dst, s_lo, r_hi, start=False, stop=last)

        def unit_ready(u, i=None):
            pe.wait_ge(w_lo_done, u + 1 if i is None else i * RING + (u + 1))

        def banks_free(g, i=None):
            if i is not None:
                pe.wait_ge(group_evac, i * RING + evacuated(g - 3))
            elif g >= 3:
                q = g - 3 - G_QKV
                if 0 <= q < N_QKV - 1:
                    pe.wait_ge(rope_raw, 2 * q + 2)
                elif q == N_QKV - 1:
                    pe.wait_ge(v_raw, TT)
                else:
                    pe.wait_ge(group_evac, evacuated(g - 3))

        def weights(u, k, b):
            s = u % RING
            return w_hi[s][:, k, b, :], w_lo[s][:, k, b, :]

        def columns(u, ks, src, b0, k_first=0, k_last=UK - 1, koff=0, signal_first=False):
            for b in range(2):
                for k in ks:
                    last = three(bank(b0 + b), *weights(u, k, b), src[0][:, k + koff, :], src[1][:, k + koff, :],
                                 k + koff == k_first, k + koff == k_last)
                if signal_first and b == 0:
                    last.then_inc(m_first, 1)
            return last

        def tokens(u, b0, fill=None):
            s = u % RING
            for t in range(TT):
                dst = ps[:, T * b0 + 256 * t:T * b0 + 256 * t + 256]
                tt = slice(P * t, P * t + P)
                if fill is not None:
                    fill(t)
                for k in range(UK):
                    r = [w[s][:, k].rearrange("p b n -> p (b n)") for w in (w_hi, w_lo)]
                    last = three(dst, hx_hi[:, k, tt], hx_lo[:, k, tt], r[0], r[1], k == 0, k == UK - 1)
            return last

        hx = (hx_hi, hx_lo)
        y = (y_hi, y_lo)
        gg = (g_hi, g_lo)

        def mean_square(n):
            if n:
                pe.wait_ge(std_done, n)
            for src, (ready, value) in ((sumsq, (sum_done, N_SUMS * (n + 1))), (sq[0], (sq_done, DT * n + DT - 1)),
                                        (sq[1], (sq_done, DT * (n + 1)))):
                pe.wait_ge(ready, value)
                for t in range(TT):
                    last = pe.matmul(bank(7)[:, t:t + 1], src[:, P * t:P * t + P], ones[:, 0:1], start=src is sumsq and t == 0, stop=src is sq[1] and t == TT - 1)
            last.then_inc(ms_mm, 1)

        def keep_clock(n, b):
            for _ in range(n):
                pe.matmul(bank(b)[:, 0:P], ones_r[:], ones_r[:], start=True, stop=True)

        def spread(n):
            pe.wait_ge(diag_done, n + 1)
            pe.matmul(bank(6), ones, diag[:].rearrange("p t c -> p (t c)"), start=True, stop=True).then_inc(bc_mm, 1)

        def first_two(u, ready, fill=None):
            for j in range(2):
                banks_free(group_of(u + j))
                if u:
                    unit_ready(u + j)
            for k in range(UK):
                ready(k)
                if fill is not None:
                    fill(k)
                for j in range(2):
                    b0 = group_banks(group_of(u + j))
                    src = y if u in U_OUT else hx
                    last = None
                    for b in range(2):
                        last = three(bank(b0 + b), *weights(u + j, k, b), src[0][:, k, :], src[1][:, k, :], k == 0, k == UK - 1)
                        if u in U_OUT and k == UK - 1 and b == 0:
                            last.then_inc(m_first, 1)
                    if k == UK - 1:
                        last.then_inc(unit_done, 1)

        def unit(u, src, i=None):
            g = group_of(u)
            banks_free(g, i)
            unit_ready(u, i)
            columns(u, range(UK), src, group_banks(g), signal_first=src is y).then_inc(unit_done, 1)

        pe.wait_ge(const_in, 16)
        pe.wait_ge(pregain_in, 16)
        pe.transpose(bank(5)[:, 0:16], vrow[0:16, 0, :], ident[0:16, 0:16]).then_inc(vec_mm, 1)

        def turn(i):
            pe.wait_ge(x_loaded[i // 2], 16)
            if i >= 2:
                pe.wait_ge(xt_copied, i - 1)
            for t in range(TT):
                last = pe.transpose(bank(6 + i % 2)[:, P * t:P * t + P], x_in[:, t, P * i:P * i + P], ident)
            last.then_inc(xt_mm, 1)

        def turn_vectors():
            pe.wait_ge(vec_in, 16 * 14)
            pe.wait_ge(vec_done, 1)
            c = 0
            for r, n in enumerate([V_ROWS0] + [4 * FT] * 4):
                last = pe.transpose(bank(5)[:, c:c + n], vrow[0:n, r, :], ident[0:n, 0:n])
                c += n
            last.then_inc(vec_mm, 1)

        turn(0)
        turn(1)

        def fill_start(k):
            if k + 2 < DT:
                turn(k + 2)
            if k == DT - 2:
                turn_vectors()
            if k == DT - 1:
                pe.wait_ge(xt_copied, DT)
                mean_square(0)

        def start_ready(k):
            pe.wait_ge(hx_ready, k + 1)
            if k % 2 == 0:
                piece_wait(pe, k, first_lo, w_lo_done)
                piece_wait(pe, k + 1, first_lo, w_lo_done)

        first_two(U_IN, start_ready, fill=fill_start)
        spread(0)
        pe.wait_ge(vec_done, 2)
        pe.wait_ge(gates_in, 64)
        for u in range(2, N_IN):
            if u < 8:
                unit(u, hx)
            elif u == 8:
                banks_free(group_of(u))
                unit_ready(u)
                tokens(u, group_banks(group_of(u))).then_inc(unit_done, 1)
            if 2 <= u < 6:
                t = u - 2
                if t == 0:
                    pe.wait_ge(rbc_done, 1)
                    pe.wait_ge(std_done, 1)
                pe.wait_ge(xc_tap, 6 * (t // 2 + 1))
                for b in range(2):
                    if t:
                        pe.wait_ge(gate_act, 2 * t - 1 + b)
                    pe.matmul(bank(6 + b), gate_w[:, b, t, :], xc[:, t, :], start=True, stop=True).then_inc(gate_mm, 1)

        def sb_z(h):
            hh = slice(HD * (h % 2), HD * (h % 2) + HD)
            if h:
                pe.wait_ge(z_copied, h)
            for j in range(TT):
                dst = ps[:, OFF[j]:OFF[j] + T - P * j]
                pe.matmul(dst, kT[hh, h // 2, P * j:P * j + P], qT[hh, h // 2, P * j:T], start=True, stop=False)
                last = pe.matmul(dst[:, 0:P], ident_b[:], mask_b[:], start=False, stop=True)
            last.then_inc(z_mm, 1)

        def sb_cum(h):
            pe.wait_ge(sp_lo_done, h + 1)
            if h:
                pe.wait_ge(t_done, h)
            for j in range(TT):
                for jj in range(j, TT):
                    n = T - P * jj
                    dst = ps[:, 3 * T + OFF[j] + P * (jj - j):3 * T + OFF[j] + P * (jj - j) + n]
                    for part in (sp_hi[h % 2], sp_lo[h % 2]):
                        last = pe.matmul(dst, (tri_r if jj == j else ones_r)[:], part[:, OFF[jj]:OFF[jj] + n],
                                         start=(jj == j and part is sp_hi[h % 2]), stop=(jj == TT - 1 and part is not sp_hi[h % 2]))
            last.then_inc(cum_mm, 1)

        def sb_av(h):
            ti, hh = h // 2, h % 2
            pe.wait_ge(w_done, h + 1)
            if ti >= 2 and hh == 0:
                pe.wait_ge(y_ready, 1 + ti - 1)
            for j in range(TT):
                n = T - P * j
                last = pe.matmul(bank(6 + ti % 2)[HD * hh:HD * hh + HD, P * j:T], v0[:, j, HD * h:HD * h + HD],
                                 z_s[h % 4][:, OFF[j]:OFF[j] + n], start=(j == 0), stop=(j == TT - 1))
            last.then_inc(av_mm, 1)

        pe.wait_ge(group_evac, N_IN - 2)
        pe.wait_ge(consts_cast, 1)
        sb_z(0)
        pe.wait_ge(gate_act, 2 * LT)
        u = N_IN - 1
        unit_ready(u)
        tokens(u, group_banks(group_of(u)), fill=lambda t: sb_z(1) if t == 2 else None).then_inc(unit_done, 1)
        pe.wait_ge(group_evac, N_IN)
        for h in range(SB_HEADS):
            sb_cum(h)
            if h + 2 < SB_HEADS:
                sb_z(h + 2)
            if h:
                sb_av(h - 1)
        sb_av(SB_HEADS - 1)

        def boundary(n, bi, u):
            mean_square(n)
            keep_clock(16, 6)
            spread(n)
            keep_clock(36, 7)
            first_two(u, lambda k: pe.wait_ge(hx_ready, DT * (bi + 1) + k + 1),
                      fill=lambda k: mean_square(n + 1) if k == DT - 1 else None)
            spread(n + 1)

        def out_projection(layer):
            first_two(U_OUT[layer], (lambda k: pe.wait_ge(y_ready, 1 if k < LT else k - LT + 2)) if layer == 0 else
                      (lambda k: pe.wait_ge(y_ready, 1 + LT + NCH)))
            for j in range(2, N_OUT):
                unit(U_OUT[layer] + j, y)

        def ffn(layer, bi):
            u0 = U_UP[layer]
            n = 4 * layer + 1
            boundary(n, bi, u0)
            for j in range(2, 5):
                unit(u0 + j, hx)
            with pe.Fori(1, 6) as i:
                for j in range(RING):
                    unit(u0 + 2 + j, hx, i=i)
            for j in range(20, FT):
                unit(u0 + j, hx)
            g_up = group_of(U_DOWN[layer])
            for mp in range(4):
                b0 = group_banks(g_up + mp)
                if layer == 0 or mp < 3:
                    banks_free(g_up + mp)
                else:
                    pe.wait_ge(mtok_done, 2)
                for c, (k0, k1) in enumerate(DOWN_K):
                    u = U_DOWN[layer] + 3 * mp + c
                    unit_ready(u)
                    pe.wait_ge(g_ready, FT * layer + k1)
                    if layer == 0:
                        columns(u, range(k1 - k0), gg, b0, k_last=FT - 1, koff=k0, signal_first=c == 2).then_inc(unit_done, 1)
                        continue
                    for t in range(TT):
                        dst = ps[:, T * b0 + 256 * t:T * b0 + 256 * t + 256]
                        tt = slice(P * t, P * t + P)
                        for k in range(k0, k1):
                            r = [w[u % RING][:, k - k0].rearrange("p b n -> p (b n)") for w in (w_hi, w_lo)]
                            last = three(dst, g_hi[:, k, tt], g_lo[:, k, tt], r[0], r[1], k == 0 and t % 2 == 0, k == FT - 1 and t % 2 == 1)
                        if c == 2 and t == 1:
                            last.then_inc(mtok_mm, 1)
                    last.then_inc(unit_done, 1)
                    if mp < 2 and c < 2:
                        for i in range(4 * mp + 2 * c, 4 * mp + 2 * c + 2):
                            if i >= 2:
                                pe.wait_ge(xtok_copied, i - 1)
                            for t in range(TT):
                                last = pe.transpose(bank(6 + i % 2)[:, P * t:P * t + P], x[:, i, P * t:P * t + P], ident)
                            last.then_inc(xtok_mm, 1)

        out_projection(0)
        ffn(0, 0)
        boundary(3, 1, U_QKV)
        for k in range(2, N_QKV):
            u = U_QKV + k
            if k < N_QKV - 1:
                unit(u, hx)

        def sw_scores(c):
            if c >= 2:
                pe.wait_ge(ex_done, c - 1)
            kw = HD if c == 0 else P
            k0 = 0 if c == 0 else CHUNK * (c - 1)
            for e in range(8):
                kv, h = e % KV, e // KV
                dst = ps[:, T * sw_banks(c) + P * e:T * sw_banks(c) + P * e + kw]
                last = pe.matmul(dst, qr[:, kv, c].rearrange("p g t -> p (g t)"), kz[h][:, kv, k0:k0 + kw], start=True, stop=True)
            last.then_inc(s_mm, 1)

        def sw_turn(c):
            kw = HD if c == 0 else P
            pe.wait_ge(pn_done, c + 1)
            if c:
                pe.wait_ge(pt_copied, 2 * c)
            for e in range(8):
                last = pe.transpose(ps[0:kw, T * 4 + P * e:T * 4 + P * e + P], prob[c % 2][:, e, 0:kw], ident)
                if e % 4 == 3:
                    last.then_inc(pt_mm, 1)

        def sw_values(c):
            pe.wait_ge(pt_copied, 2 * (c + 1))
            if c >= 2:
                pe.wait_ge(y_ready, 1 + LT + c - 1)
            if c == 2:
                pe.wait_ge(v_shift, 32)
            kw = HD if c == 0 else P
            v = v1[0:HD, 0] if c == 0 else (v1[:, (c - 1) // 2] if c % 2 else v1s[:, c // 2])
            for e in range(8):
                kv, h = e % KV, e // KV
                dst = bank(6 + c % 2)[HD * h:HD * h + HD, P * kv:P * kv + P]
                last = pe.matmul(dst, v[:, HD * kv:HD * kv + HD], probT[c % 2][0:kw, e, :], start=True, stop=True)
            last.then_inc(o_mm, 1)

        def first_scores():
            pe.wait_ge(kz_zeroed, 2)
            pe.wait_ge(k_copied, 64)
            pe.wait_ge(rope_done, 12)
            sw_scores(0)

        u = U_QKV + N_QKV - 1
        banks_free(group_of(u))
        unit_ready(u)
        tokens(u, group_banks(group_of(u)), fill=lambda t: first_scores() if t == TT - 1 else None).then_inc(unit_done, 1)
        pe.wait_ge(v_raw, TT)
        sw_scores(1)
        for c in range(NCH):
            sw_turn(c)
            if c:
                sw_values(c - 1)
            if c + 2 < NCH:
                sw_scores(c + 2)
        sw_values(NCH - 1)

        out_projection(1)
        ffn(1, 2)

    es.close()


_INS = ["x", "positions", "even_w_in", "even_conv_w", "even_conv_b", "lru_w_a", "lru_b_a", "lru_w_x", "lru_b_x",
        "lru_lambda", "even_w_out", "odd_w_qkv", "odd_sinks", "odd_w_o", "ffn_w_up", "ffn_conv_w", "ffn_conv_b",
        "ffn_w_down", "norm_mix_pre", "norm_mix_post", "norm_ffn_pre", "norm_ffn_post"]


def _consts():
    c = np.zeros((P, 4 * P + 2), np.float32)
    s, t = np.arange(P)[:, None], np.arange(P)[None, :]
    c[:, 0:P] = s == t
    c[:, P:2 * P] = 1.0
    c[:, 2 * P:3 * P] = s >= t
    c[:, 3 * P:4 * P] = np.where(s >= t, MASKED, 0.0)
    half = HD // 2
    c[:, 4 * P] = (10000.0 ** (-np.arange(half) / half)).astype(np.float32)[np.arange(P) % half]
    c[:, 4 * P + 1] = np.where(np.arange(P) % HD < half, -1.0, 1.0)
    return c


def kernel(**inputs):
    import concourse.bacc as bacc
    from concourse.bass_utils import run_bass_kernel_spmd

    nc = bacc.Bacc("TRN2", target_bir_lowering=False, num_devices=1)
    arrays, io = {}, {}
    for name in _INS + ["consts"]:
        a = _consts() if name == "consts" else np.ascontiguousarray(inputs[name])
        arrays[f"in_{name}"] = a
        io[name] = nc.dram_tensor(f"in_{name}", a.shape, mybir.dt.from_np(a.dtype), kind="ExternalInput").ap()
    out = nc.dram_tensor("out", (1, T, D), F32, kind="ExternalOutput").ap()
    build(nc, io, out)
    r = run_bass_kernel_spmd(nc, [arrays], core_ids=[0])
    return r.results[0]["out"]
```
